# Optimizing a Trainium2 kernel written in Bass

```python
import math
import jax, jax.numpy as jnp
from jax import lax
import numpy as np

D_MODEL = 2048
BATCH = 1
SEQ = 256
DEPTH = 1

CHUNK = 64
EPS = 1e-6
NEG_INF = -1e30
D_MIX = D_MODEL
SSD_HEADS = 16
SSD_HEAD_DIM = (D_MIX // 2) // SSD_HEADS
D_SSD = SSD_HEADS * SSD_HEAD_DIM
SSD_GROUPS = 2
D_STATE = 128
CONV_WIDTH = 4
CONV_DIM = D_SSD + 2 * SSD_GROUPS * D_STATE
ATT_HEADS = 16
ATT_KV_HEADS = 2
ATT_HEAD_DIM = (D_MIX - D_SSD) // ATT_HEADS
D_ATT = ATT_HEADS * ATT_HEAD_DIM
D_KV = ATT_KV_HEADS * ATT_HEAD_DIM
WINDOW = 128
WINDOW_CHUNKS = WINDOW // CHUNK
IN_SPLITS = (D_SSD, D_SSD + CONV_DIM, D_SSD + CONV_DIM + SSD_HEADS,
             D_SSD + CONV_DIM + SSD_HEADS + D_ATT,
             D_SSD + CONV_DIM + SSD_HEADS + D_ATT + D_KV)
IN_PROJ_DIM = D_SSD + CONV_DIM + SSD_HEADS + D_ATT + 2 * D_KV
PEER_HEADS = 8
PEER_N_KEYS = 128
PEER_N_EXPERTS = PEER_N_KEYS * PEER_N_KEYS
PEER_QUERY_DIM = 256
PEER_HALF = PEER_QUERY_DIM // 2
PEER_TOPK = 16
PEER_TOKEN_BLOCK = 128

kernel_name = "hybrid_ssd_swa_sink_peer_block"

def rmsnorm(x, g):
    xf = x.astype(jnp.float32)
    y = xf * lax.rsqrt(jnp.mean(xf * xf, axis=-1, keepdims=True) + EPS)
    return (y * g.astype(jnp.float32)).astype(x.dtype)

def causal_depthwise_conv(u, w, b):
    c = u.shape[-1]
    y = lax.conv_general_dilated(u, w[:, None, :].astype(u.dtype), window_strides=(1,),
                                 padding=[(CONV_WIDTH - 1, 0)],
                                 dimension_numbers=("NWC", "WIO", "NWC"),
                                 feature_group_count=c)
    return y + b.astype(u.dtype)

def ssd_scan(xs, bs, cs, dt, a_log, d_skip):
    f32 = jnp.float32
    b, s = xs.shape[:2]
    nc = s // CHUNK
    r = SSD_HEADS // SSD_GROUPS
    xs, bs, cs, dt = (t.astype(f32) for t in (xs, bs, cs, dt))
    a_head = -jnp.exp(a_log.astype(f32))
    a = (dt * a_head).reshape(b, nc, CHUNK, SSD_GROUPS, r)
    a = jnp.transpose(a, (0, 3, 4, 1, 2))
    a_cs = jnp.cumsum(a, axis=-1)
    xdt = (xs * dt[..., None]).reshape(b, nc, CHUNK, SSD_GROUPS, r, SSD_HEAD_DIM)
    bc = bs.reshape(b, nc, CHUNK, SSD_GROUPS, D_STATE)
    cc = cs.reshape(b, nc, CHUNK, SSD_GROUPS, D_STATE)
    tri = jnp.tril(jnp.ones((CHUNK, CHUNK), dtype=bool))
    seg = a_cs[..., :, None] - a_cs[..., None, :]
    lmat = jnp.exp(jnp.where(tri, seg, NEG_INF))
    cb = jnp.einsum("bclgn,bcsgn->bgcls", cc, bc)
    y_diag = jnp.einsum("bgrcls,bcsgrp->bclgrp", cb[:, :, None] * lmat, xdt)
    decay_states = jnp.exp(a_cs[..., -1:] - a_cs)
    states = jnp.einsum("bclgn,bgrcl,bclgrp->bcgrpn", bc, decay_states, xdt)
    chunk_decay = jnp.exp(a_cs[..., -1])

    def step(h, inp):
        st, dec = inp
        return h * dec[..., None, None] + st, h

    h0 = jnp.zeros_like(states[:, 0])
    _, prev = lax.scan(step, h0, (jnp.moveaxis(states, 1, 0), jnp.moveaxis(chunk_decay, -1, 0)))
    prev = jnp.moveaxis(prev, 0, 1)
    y_off = jnp.einsum("bclgn,bcgrpn,bgrcl->bclgrp", cc, prev, jnp.exp(a_cs))
    y = (y_diag + y_off).reshape(b, s, SSD_HEADS, SSD_HEAD_DIM)
    return y + d_skip.astype(f32)[:, None] * xs

def swa_sink_attention(q, k, v, sinks):
    f32 = jnp.float32
    b, s = q.shape[:2]
    nc = s // CHUNK
    r = ATT_HEADS // ATT_KV_HEADS
    qc = q.astype(f32).reshape(b, nc, CHUNK, ATT_KV_HEADS, r, ATT_HEAD_DIM)
    kc = k.astype(f32).reshape(b, nc, CHUNK, ATT_KV_HEADS, ATT_HEAD_DIM)
    vc = v.astype(f32).reshape(b, nc, CHUNK, ATT_KV_HEADS, ATT_HEAD_DIM)
    pad = ((0, 0), (WINDOW_CHUNKS - 1, 0), (0, 0), (0, 0), (0, 0))
    kp = jnp.pad(kc, pad)
    vp = jnp.pad(vc, pad)
    kw = jnp.concatenate([kp[:, j:j + nc] for j in range(WINDOW_CHUNKS)], axis=2)
    vw = jnp.concatenate([vp[:, j:j + nc] for j in range(WINDOW_CHUNKS)], axis=2)
    logits = jnp.einsum("bclkrd,bcmkd->bkrclm", qc, kw) * (ATT_HEAD_DIM ** -0.5)
    key_chunk = (jnp.arange(nc)[:, None] - (WINDOW_CHUNKS - 1)
                 + jnp.arange(WINDOW_CHUNKS * CHUNK)[None, :] // CHUNK)
    logits = jnp.where((key_chunk >= 0)[:, None, :], logits, NEG_INF)
    sink = jnp.broadcast_to(sinks.astype(f32).reshape(ATT_KV_HEADS, r)[None, :, :, None, None, None],
                            logits.shape[:-1] + (1,))
    p = jax.nn.softmax(jnp.concatenate([logits, sink], axis=-1), axis=-1)[..., :-1]
    o = jnp.einsum("bkrclm,bcmkd->bclkrd", p, vw)
    return o.reshape(b, s, D_ATT)

def peer_ffn(xn, wq, keys, u_tab, v_tab):
    f32 = jnp.float32
    b, s, d = xn.shape
    t = b * s
    xf = xn.reshape(t, d)
    q = (xf @ wq).reshape(t, PEER_HEADS, 2, PEER_HALF)
    sc = jnp.einsum("thpk,hpnk->thpn", q.astype(f32), keys.astype(f32))
    s1, i1 = lax.top_k(sc[:, :, 0], PEER_TOPK)
    s2, i2 = lax.top_k(sc[:, :, 1], PEER_TOPK)
    cand = (s1[..., :, None] + s2[..., None, :]).reshape(t, PEER_HEADS, PEER_TOPK * PEER_TOPK)
    cidx = (i1[..., :, None] * PEER_N_KEYS + i2[..., None, :]).reshape(t, PEER_HEADS, PEER_TOPK * PEER_TOPK)
    top, pos = lax.top_k(cand, PEER_TOPK)
    eidx = jnp.take_along_axis(cidx, pos, axis=-1)
    gate = jax.nn.softmax(top, axis=-1).astype(xn.dtype)
    nb = t // PEER_TOKEN_BLOCK

    def block(args):
        xb, ib, gb = args
        u = jnp.take(u_tab, ib, axis=0)
        act = jax.nn.gelu(jnp.einsum("thkd,td->thk", u, xb), approximate=False)
        v = jnp.take(v_tab, ib, axis=0)
        return jnp.einsum("thk,thkd->td", gb * act, v)

    out = lax.map(block, (xf.reshape(nb, PEER_TOKEN_BLOCK, d),
                          eidx.reshape(nb, PEER_TOKEN_BLOCK, PEER_HEADS, PEER_TOPK),
                          gate.reshape(nb, PEER_TOKEN_BLOCK, PEER_HEADS, PEER_TOPK)))
    return out.reshape(b, s, d)

def setup_inputs(seed: int = 0) -> dict:
    key = jax.random.key(seed)
    ks = jax.random.split(key, 18)
    f32 = jnp.float32
    nl = DEPTH

    def nrm(k, shape, scale):
        return jax.random.normal(k, shape, f32) * scale

    def gain(k, shape):
        return 1.0 + 0.02 * jax.random.normal(k, shape, f32)

    dt0 = jnp.exp(jax.random.uniform(ks[5], (nl, SSD_HEADS), f32, math.log(1e-3), math.log(1e-1)))
    return {
        "x": nrm(ks[0], (BATCH, SEQ, D_MODEL), 1.0),
        "norm1_g": gain(ks[1], (nl, D_MODEL)),
        "w_in": nrm(ks[2], (nl, D_MODEL, IN_PROJ_DIM), D_MODEL ** -0.5),
        "conv_w": nrm(ks[3], (nl, CONV_WIDTH, CONV_DIM), CONV_WIDTH ** -0.5),
        "conv_b": nrm(ks[4], (nl, CONV_DIM), 0.02),
        "dt_bias": dt0 + jnp.log(-jnp.expm1(-dt0)),
        "a_log": jnp.log(jax.random.uniform(ks[6], (nl, SSD_HEADS), f32, 1.0, 16.0)),
        "d_skip": gain(ks[7], (nl, SSD_HEADS)),
        "ssd_norm_g": gain(ks[8], (nl, D_SSD)),
        "attn_sinks": nrm(ks[9], (nl, ATT_HEADS), 0.5),
        "attn_norm_g": gain(ks[10], (nl, D_ATT)),
        "w_out": nrm(ks[11], (nl, D_MIX, D_MODEL), D_MIX ** -0.5),
        "norm2_g": gain(ks[12], (nl, D_MODEL)),
        "peer_wq": nrm(ks[13], (nl, D_MODEL, PEER_HEADS * PEER_QUERY_DIM), D_MODEL ** -0.5),
        "peer_keys": nrm(ks[14], (nl, PEER_HEADS, 2, PEER_N_KEYS, PEER_HALF), PEER_HALF ** -0.5),
        "peer_u": nrm(ks[15], (nl, PEER_N_EXPERTS, D_MODEL), D_MODEL ** -0.5),
        "peer_v": nrm(ks[16], (nl, PEER_N_EXPERTS, D_MODEL), PEER_HEADS ** -0.5),
        "norm_f_g": gain(ks[17], (D_MODEL,)),
    }

def reference(x, norm1_g, w_in, conv_w, conv_b, dt_bias, a_log, d_skip, ssd_norm_g,
              attn_sinks, attn_norm_g, w_out, norm2_g, peer_wq, peer_keys, peer_u, peer_v,
              norm_f_g):
    b, s, _ = x.shape
    h = x
    for i in range(DEPTH):
        xn = rmsnorm(h, norm1_g[i])
        proj = xn @ w_in[i]
        z, xbc, dt_raw, q, k, v = jnp.split(proj, list(IN_SPLITS), axis=-1)
        xbc = jax.nn.silu(causal_depthwise_conv(xbc, conv_w[i], conv_b[i]))
        xs, bs, cs = jnp.split(xbc, [D_SSD, D_SSD + SSD_GROUPS * D_STATE], axis=-1)
        dt = jax.nn.softplus(dt_raw.astype(jnp.float32) + dt_bias[i].astype(jnp.float32))
        y_ssd = ssd_scan(xs.reshape(b, s, SSD_HEADS, SSD_HEAD_DIM),
                         bs.reshape(b, s, SSD_GROUPS, D_STATE),
                         cs.reshape(b, s, SSD_GROUPS, D_STATE), dt, a_log[i], d_skip[i])
        y_ssd = y_ssd.reshape(b, s, D_SSD) * jax.nn.silu(z.astype(jnp.float32))
        y_ssd = rmsnorm(y_ssd.reshape(b, s, SSD_GROUPS, D_SSD // SSD_GROUPS),
                        ssd_norm_g[i].reshape(SSD_GROUPS, D_SSD // SSD_GROUPS))
        y_ssd = y_ssd.reshape(b, s, D_SSD).astype(x.dtype)
        y_att = swa_sink_attention(q.reshape(b, s, ATT_HEADS, ATT_HEAD_DIM),
                                   k.reshape(b, s, ATT_KV_HEADS, ATT_HEAD_DIM),
                                   v.reshape(b, s, ATT_KV_HEADS, ATT_HEAD_DIM), attn_sinks[i])
        y_att = rmsnorm(y_att, attn_norm_g[i]).astype(x.dtype)
        h = h + jnp.concatenate([y_ssd, y_att], axis=-1) @ w_out[i]
        h = h + peer_ffn(rmsnorm(h, norm2_g[i]), peer_wq[i], peer_keys[i], peer_u[i], peer_v[i])
    return rmsnorm(h, norm_f_g)


_drawn_inputs = setup_inputs


def setup_inputs(seed=0):
    import zlib

    import numpy as np

    out = dict(_drawn_inputs(seed))
    spreads = {}
    factors = {'conv_b': 2.71,
     'd_skip': 18.557,
     'ssd_norm_g': 12.06,
     'attn_sinks': 8.0,
     'attn_norm_g': 11.344,
     'norm2_g': 10.62,
     'norm_f_g': 7.97}
    for name, (base, spread) in spreads.items():
        noise = np.random.default_rng([zlib.crc32(name.encode()), seed]).standard_normal(out[name].shape)
        drawn = base * np.exp(spread * noise) if base else spread * noise
        out[name] = __import__('jax').numpy.asarray(drawn.astype(out[name].dtype))
    for name, factor in factors.items():
        out[name] = (out[name] * factor).astype(out[name].dtype)
    return out
```

```python
from contextlib import ExitStack

import concourse.bass as bass
from concourse import mybir

F32 = mybir.dt.float32
F32R = mybir.dt.float32r
U32 = mybir.dt.uint32
ALU = mybir.AluOpType
ACT = mybir.ActivationFunctionType
AX = mybir.AxisListType.X
ds = bass.ds

P = 128
T = 256
D = 2048
KT = D // P
TB = T // P
SSD_HEADS, HEAD_DIM, GROUPS = 16, 64, 2
D_SSD = SSD_HEADS * HEAD_DIM
SSD_TILES = D_SSD // P
CONV_W = 4
CONV_TILES = SSD_TILES + 2 * GROUPS
PEER_HEADS, TOPK, N_KEYS = 8, 16, 128
EPS = 1e-6
LOWEST = -3.0e38
BLK = T + P

N_IN = 1 + CONV_TILES + 2 + 2 * SSD_TILES
C_DT, C_CONV, C_K, C_V, C_QZ = 0, 1, 1 + CONV_TILES, 2 + CONV_TILES, 3 + CONV_TILES
C_OUT = N_IN
C_WQ = C_OUT + KT
C_U = C_WQ + 2 * PEER_HEADS
C_V_TAB = C_U + N_KEYS
C_END = C_V_TAB + N_KEYS
ROUTE_STEPS = TB * PEER_HEADS
TOK_GROUP = 4
GATE_CHUNKS = T // TOK_GROUP
PIECE = 1024
RING = 4

_small = {}
_at = 0
for _name, _n in (("ones", P), ("tri", BLK), ("window", BLK), ("g1", KT), ("g_mix", KT), ("g2", KT),
                  ("d_skip", SSD_TILES), ("conv_w", CONV_TILES * CONV_W), ("conv_b", CONV_TILES),
                  ("dt_bias", 1), ("a_log", 1), ("sinks", 2 * SSD_TILES)):
    _small[_name] = (_at, _n)
    _at += _n
SMALL = _at


class Order:

    def __init__(self, eng, sem):
        self.eng, self.sem, self.n, self.here = eng, sem, 0, 0

    def step(self, ins):
        ins.then_inc(self.sem, 1)
        self.n = self.n + 1
        self.here += 1

    def settle(self):
        self.eng.wait_ge(self.sem, self.n)

    def enter(self, i, per):
        self.base, self.per, self.here = self.n, per, 0
        self.n = self.base + i * per

    def leave(self, rounds):
        assert self.here == self.per, (self.here, self.per)
        self.n = self.base + rounds * self.per


def build(nc, x_t, small, id_iota, w_in, w_out, w_q, keys, u_tab, v_tab, g_f, out):
    h_scratch = nc.dram_tensor("h_scratch", (P, KT * T), F32).ap()
    gelu_scratch = nc.dram_tensor("gelu_scratch", (N_KEYS, P, T), F32).ap()

    with ExitStack() as ctx:
        def sb(stack, name, cols, dt=F32):
            return stack.enter_context(nc.sbuf_tensor(name, [P, cols], dt))

        def sem(name):
            return ctx.enter_context(nc.semaphore(name))

        raw = sb(ctx, "raw", RING * PIECE)
        high = sb(ctx, "high", RING * PIECE, F32R)
        low = sb(ctx, "low", RING * PIECE, F32R)
        big = sb(ctx, "big", N_KEYS * T)
        side = sb(ctx, "side", 1536)
        consts = sb(ctx, "consts", 2 * P)
        ident, iota = consts[:, 0:P], consts[:, P:2 * P]
        with ExitStack() as early:
            act_hi = sb(early, "act_hi", KT * T, F32R)
            act_lo = sb(early, "act_lo", KT * T, F32R)
            pick_t = sb(early, "pick_t", 3 * T)
        h_back = sb(ctx, "h_back", KT * T)
        g_last = sb(ctx, "g_last", D)
        sb(ctx, "unused", KT * T - D)
        w_hi = sb(ctx, "w_hi", 2 * T, F32R)
        w_lo = sb(ctx, "w_lo", 2 * T, F32R)
        ps = ctx.enter_context(nc.psum_tensor("ps", [P, 8, 512], F32))

        def view(at, cols):
            return big[:, at:at + cols]

        X_T, H_T, Y_T, SQ, XN = 0, 4096, 8192, 12288, 16384
        x_sb, h_sb, y_sb, sq_sb, xn_sb = (view(a, KT * T) for a in (X_T, H_T, Y_T, SQ, XN))
        UP = CONV_W - 1 + T + 1
        CONV_IN, XBC = 20480, 20480 + CONV_TILES * UP
        QZ = XBC + CONV_TILES * T
        conv_in = view(CONV_IN, CONV_TILES * UP).rearrange("p (c u) -> p c u", u=UP)
        X_TOK = H_T
        x_tok = view(X_TOK, TB * D_SSD)
        E_AT = H_T + TB * D_SSD
        expo = [view(E_AT + k * BLK, BLK) for k in range(2)]
        m_sb = [view(E_AT + (2 + k) * BLK, BLK) for k in range(2)]
        xdt = [view(E_AT + 4 * BLK + k * P, P) for k in range(2)]
        TAIL = QZ + KT * T
        cb_m = [view(TAIL + g * BLK, BLK) for g in range(GROUPS)]
        k_t = view(TAIL + 2 * BLK, T)
        v_t = view(TAIL + 2 * BLK + T, T)
        v_tok = view(TAIL + 2 * BLK + 2 * T, TB * P)
        tok_t = view(TAIL + 2 * BLK + 3 * T, 4 * SSD_HEADS)
        assert TAIL + 2 * BLK + 3 * T + 4 * SSD_HEADS <= N_KEYS * T
        cs_rows = view(SQ, SSD_HEADS * BLK)
        DT = SQ + SSD_HEADS * BLK
        dtv = [big[0:SSD_HEADS, DT + k * T:DT + (k + 1) * T] for k in range(6)]
        cs = big[0:SSD_HEADS, DT + 6 * T:DT + 6 * T + BLK]
        decay = big[0:SSD_HEADS, DT + 6 * T + BLK:DT + 6 * T + BLK + 1]
        assert 6 * T + BLK + 1 <= 2048
        q_in = [view(SQ + k * T, T) for k in range(2)]
        A2 = SQ + 2 * T
        prob = [view(A2 + k * 2 * BLK, 2 * BLK).rearrange("p (e m) -> p e m", e=2) for k in range(2)]
        A3 = A2 + 4 * BLK
        prob_t = [view(A3 + k * 2 * BLK, 2 * BLK).rearrange("p (e m) -> p e m", e=2) for k in range(2)]
        A4 = A3 + 4 * BLK
        st = [[view(A4 + (k * 5 + m) * 4, 4) for m in range(5)] for k in range(2)]
        key_t = view(CONV_IN, 2 * PEER_HEADS * N_KEYS)
        SCORES = QZ
        q_t = [view(XBC + k * T, T) for k in range(2)]
        r_s, r_s2 = (view(k * 256, 256).rearrange("p (s n) -> p s n", s=2) for k in range(2))
        r_c, r_c2 = (view(512 + k * 256, 256) for k in range(2))
        r_eq = [view(1024 + k * 256, 256).rearrange("p (k a) -> p k a", a=TOPK) for k in range(2)]
        r_v = view(1536, 2 * TOPK)
        r_ix = view(1568, 2 * TOPK).bitcast(U32)
        r_ixf = view(1600, 2 * TOPK)
        r_tv = view(1632, TOPK)
        r_tp = view(1648, TOPK).bitcast(U32)
        r_ab = [view(1664 + k * TOPK, TOPK).bitcast(U32) for k in range(2)]
        PICKS = 2048
        pick = [view(PICKS + k * 256, 256) for k in range(3)]
        r_sum = view(2816, ROUTE_STEPS)
        r_mark = view(2816 + ROUTE_STEPS, 1)
        rs_v, rs_r = (view(XBC + (2 + 3 * k) * T, 3 * T) for k in range(2))

        def sm(name, lo=0, n=None):
            at, size = _small[name]
            return side[:, at + lo:at + lo + (size if n is None else n)]

        gelu_out = [side[:, k * T:(k + 1) * T] for k in range(2)]
        hot_col = side[:, 2 * T:2 * T + TOK_GROUP * P]
        hot_row = side[:, 4 * T:4 * T + TOK_GROUP * P]
        gelu_in = [side[:, (2 + k) * T:(3 + k) * T] for k in range(2)]
        w_full = [side[:, (4 + k) * T:(5 + k) * T] for k in range(2)]

        small_in = sem("small_in")
        consts_in = sem("consts_in")
        x_in = [sem(f"x_in{k}") for k in range(4)]
        keys_in = sem("keys_in")
        raw_in = [sem(f"raw_in{k}") for k in range(RING)]
        hi_done = sem("hi_done")
        lo_done = sem("lo_done")
        used = sem("used")
        taken = sem("taken")
        squared = sem("squared")
        summed = sem("summed")
        var_ok = sem("var_ok")
        root_ok = sem("root_ok")
        xn_ok = sem("xn_ok")
        xh_ok = sem("xh_ok")
        xl_ok = sem("xl_ok")
        dve_own = sem("dve_own")
        pads_ok = sem("pads_ok")
        conv_ok = sem("conv_ok")
        silu_ok = sem("silu_ok")
        dt_neg = sem("dt_neg")
        dt_exp = sem("dt_exp")
        cs_ok = sem("cs_ok")
        rows_ok = sem("rows_ok")
        tr_ok = sem("tr_ok")
        tok_ok = sem("tok_ok")
        cb_ok = sem("cb_ok")
        cbm_ok = sem("cbm_ok")
        small_t = sem("small_t")
        bc_ok = sem("bc_ok")
        seg_ok = sem("seg_ok")
        exp_ok = sem("exp_ok")
        m_ok = sem("m_ok")
        y_ok = sem("y_ok")
        y_out = sem("y_out")
        z_ok = sem("z_ok")
        q_ok = sem("q_ok")
        logit_ok = sem("logit_ok")
        max_ok = sem("max_ok")
        p_ok = sem("p_ok")
        pn_ok = sem("pn_ok")
        pt_ok = sem("pt_ok")
        pt_out = sem("pt_out")
        o_ok = sem("o_ok")
        o_out = sem("o_out")
        mix_ok = sem("mix_ok")
        score_ok = sem("score_ok")
        score_out = sem("score_out")
        h_saved = sem("h_saved")
        soft_in = sem("soft_in")
        soft_exp = sem("soft_exp")
        picks_ok = sem("picks_ok")
        picks_tr = sem("picks_tr")
        hot_ok = sem("hot_ok")
        gate_ok = sem("gate_ok")
        gate_out = sem("gate_out")
        gelu_saved = [sem(f"gelu_saved{k}") for k in range(2)]
        gelu_back = [sem(f"gelu_back{k}") for k in range(2)]
        w_ok = sem("w_ok")
        wh_ok = sem("wh_ok")
        wl_ok = sem("wl_ok")
        h_in = sem("h_in")
        gf_in = sem("gf_in")
        sum_ok = sem("sum_ok")
        last_sq = sem("last_sq")
        last_var = sem("last_var")
        last_root = sem("last_root")
        last_ok = sem("last_ok")
        stored = sem("stored")

        def slot(t, s):
            return t[:, s * PIECE:(s + 1) * PIECE]

        block = ctx.enter_context(nc.Block())

        @block.sync
        def _(sp):
            def load(c, par, src):
                for half in range(2):
                    s = 2 * par + half
                    if not (isinstance(c, int) and c < 2):
                        sp.wait_ge(lo_done, 2 * c + half - 3)
                    sp.dma_start(slot(raw, s), src[:, half * PIECE:(half + 1) * PIECE]).then_inc(raw_in[s], 16)

            def load_all(tab, first, count, extra=None):
                with sp.Fori(0, count // 2) as i:
                    for j in range(2):
                        load(first + 2 * i + j, (first + j) % 2, tab[2 * i + j])
                        if extra:
                            extra(2 * i + j, (first + j) % 2)
                if count % 2:
                    load(first + count - 1, (first + count - 1) % 2, tab[count - 1])

            sp.dma_start(side[:, 0:SMALL], small).then_inc(small_in, 16)
            for k in range(4):
                sp.dma_start(x_sb[:, k * 4 * T:(k + 1) * 4 * T], x_t[:, k * 4 * T:(k + 1) * 4 * T]).then_inc(x_in[k], 16)
            load(0, 0, w_in[0])
            sp.dma_start(consts[:, :], id_iota).then_inc(consts_in, 16)
            load(1, 1, w_in[1])
            load_all(w_in[2:N_IN], 2, N_IN - 2)
            sp.wait_ge(conv_ok, CONV_TILES)
            sp.dma_start(key_t, keys).then_inc(keys_in, 16)
            load_all(w_out, C_OUT, KT)
            load_all(w_q, C_WQ, 2 * PEER_HEADS)
            sp.wait_ge(taken, C_WQ)
            sp.dma_start(h_scratch, h_sb).then_inc(h_saved, 16)

            def save_gelu(e, par):
                sp.wait_ge(taken, C_U + 1 + e)
                sp.dma_start(gelu_scratch[e], gelu_out[par]).then_inc(gelu_saved[par], 16)

            LAG = 3
            for e in range(LAG + 1):
                load(C_U + e, (C_U + e) % 2, u_tab[e])
            with sp.Fori(0, (N_KEYS - LAG - 1) // 2) as i:
                for j in range(2):
                    e = 2 * i + j
                    save_gelu(e, (C_U + j) % 2)
                    load(C_U + LAG + 1 + e, (C_U + LAG + 1 + j) % 2, u_tab[LAG + 1 + 2 * i + j])
            for j in range(2):
                save_gelu(N_KEYS - LAG - 1 + j, (C_U + LAG + 1 + j) % 2)
                load(C_V_TAB + j, (C_V_TAB + j) % 2, v_tab[j])
            for e in range(N_KEYS - LAG + 1, N_KEYS):
                save_gelu(e, (C_U + e) % 2)
            sp.wait_ge(gate_ok, GATE_CHUNKS)
            for k in range(2):
                sp.wait_ge(gelu_saved[k], 16 * (N_KEYS // 2))

            def gelu_load(e, par):
                sp.dma_start(gelu_in[par], gelu_scratch[e]).then_inc(gelu_back[par], 16)

            for j in range(2):
                gelu_load(j, (C_V_TAB + j) % 2)
            sp.wait_ge(used, 2 * C_V_TAB)
            sp.dma_start(h_back[:, :], h_scratch).then_inc(h_in, 16)
            sp.dma_start(g_last[:, :], g_f).then_inc(gf_in, 16)
            with sp.Fori(0, N_KEYS // 2 - 1) as i:
                for j in range(2):
                    par = (C_V_TAB + j) % 2
                    load(C_V_TAB + 2 + 2 * i + j, par, v_tab[2 * i + j + 2])
                    sp.wait_ge(w_ok, 2 * i + j + 1)
                    gelu_load(2 * i + j + 2, par)
            for tb in range(TB):
                for q in range(2):
                    sp.wait_ge(last_ok, 2 * tb + q + 1)
                    n = D // 2
                    sp.dma_start(out[tb * P:(tb + 1) * P, q * n:(q + 1) * n],
                                 big[:, (2 * tb + q) * n:(2 * tb + q + 1) * n]).then_inc(stored, 16)
            sp.wait_ge(stored, 16 * 2 * TB)

        @block.gpsimd
        def _(pool):
            pool.wait_ge(cs_ok, 1)
            pool.wait_ge(consts_in, 16)
            h16 = SSD_HEADS
            nc.gpsimd.tensor_tensor(
                out=cs_rows[0:h16, :].rearrange("p (h m) -> p h m", h=h16),
                in0=cs.rearrange("p (o m) -> p o m", o=1).broadcast_to([h16, h16, BLK]),
                in1=ident[0:h16, 0:h16].rearrange("p (h o) -> p h o", o=1).broadcast_to([h16, h16, BLK]),
                op=ALU.mult).then_inc(rows_ok, 1)

        @block.scalar
        def _(act):
            def cut_high(c, par):
                for half in range(2):
                    s = 2 * par + half
                    act.wait_ge(raw_in[s], 16 * ((c - par) // 2 + 1) if isinstance(c, int) else 8 * (c - par) + 16)
                    if not (isinstance(c, int) and c < 2):
                        act.wait_ge(used, 2 * c + half - 3)
                    nc.scalar.activation(slot(high, s), slot(raw, s), ACT.Copy).then_inc(hi_done, 1)

            def take(c, par, dst, func=ACT.Copy, rows=P):
                act.wait_ge(used, 2 * c + 2)
                nc.scalar.activation(dst, ps[0:rows, par, 0:T], func).then_inc(taken, 1)

            def root(k, v, r):
                act.wait_ge(var_ok, k + 1)
                nc.scalar.activation(r, v, ACT.Sqrt).then_inc(root_ok, 1)

            def round_norm(k):
                for q in range(4):
                    act.wait_ge(xn_ok, 4 * k + q + 1)
                    a, b = q * 4 * T, (q + 1) * 4 * T
                    nc.scalar.activation(act_hi[:, a:b], xn_sb[:, a:b], ACT.Copy).then_inc(xh_ok, 1)

            for q in range(4):
                act.wait_ge(x_in[q], 16)
                a, b = q * 4 * T, (q + 1) * 4 * T
                nc.scalar.activation(sq_sb[:, a:b], x_sb[:, a:b], ACT.Square).then_inc(squared, 1)
            cut_high(0, 0)
            root(0, rs_v[:, 0:T], rs_r[:, 0:T])
            round_norm(0)
            cut_high(1, 1)
            act.wait_ge(xl_ok, 4)
            take(0, 0, dtv[0], rows=SSD_HEADS)
            act.wait_ge(small_in, 16)
            nc.scalar.activation(decay, sm("a_log")[0:SSD_HEADS], ACT.Exp).then_inc(dt_exp, 1)
            act.wait_ge(dt_neg, 1)
            nc.scalar.activation(dtv[2], dtv[1], ACT.Exp).then_inc(dt_exp, 1)
            with act.Fori(0, CONV_TILES // 2) as i:
                for j in range(2):
                    c, par = C_CONV + 2 * i + j, (C_CONV + j) % 2
                    cut_high(c + 1, 1 - par)
                    take(c, par, big[:, ds(CONV_IN + CONV_W - 1 + (2 * i + j) * UP, T)])
            cut_high(C_K + 1, (C_K + 1) % 2)
            take(C_K, C_K % 2, k_t)
            act.wait_ge(conv_ok, CONV_TILES)
            bc = view(XBC + SSD_TILES * T, 2 * GROUPS * T)
            nc.scalar.activation(bc, bc, ACT.Silu).then_inc(silu_ok, 1)
            xs = view(XBC, SSD_TILES * T)
            nc.scalar.activation(xs, xs, ACT.Silu).then_inc(silu_ok, 1)
            cut_high(C_V + 1, (C_V + 1) % 2)
            take(C_V, C_V % 2, v_t)
            for b in range(4):
                act.wait_ge(tr_ok, b + 1)
                nc.scalar.activation(x_tok[:, b * 512:(b + 1) * 512], ps[:, 4 + b, :], ACT.Copy).then_inc(tok_ok, 1)

            def ssd_step(h, j):
                c, par = C_QZ + h, (C_QZ + j) % 2
                cut_high(c + 1, 1 - par)
                take(c, par, big[:, ds(QZ + h * T, T)])
                act.wait_ge(seg_ok, h + 1)
                nc.scalar.activation(expo[j], expo[j], ACT.Exp).then_inc(exp_ok, 1)

            with act.Fori(0, SSD_HEADS // 2) as i:
                for j in range(2):
                    ssd_step(2 * i + j, j)
            z = view(QZ + SSD_TILES * T, SSD_TILES * T)
            act.wait_ge(taken, C_OUT)
            nc.scalar.activation(z, z, ACT.Silu).then_inc(z_ok, 1)

            act.wait_ge(y_out, SSD_HEADS)
            with act.Fori(0, 4) as i:
                for j in range(2):
                    pair = 2 * i + j
                    nc.scalar.activation(q_in[j], big[:, ds(QZ + pair * T, T)], ACT.Copy,
                                         scale=float(HEAD_DIM) ** -0.5).then_inc(q_ok, 1)
                    act.wait_ge(max_ok, pair + 1)
                    neg, den, snk = st[j][1], st[j][2], st[j][3]
                    for e in range(2):
                        for b, (lo, hi) in enumerate(((0, P), (P, BLK))):
                            n = 2 * b + e
                            nc.scalar.activation(prob[j][:, e, lo:hi], prob[j][:, e, lo:hi], ACT.Exp,
                                                 bias=neg[:, n:n + 1], accum_out=den[:, n:n + 1])
                    nc.scalar.activation(snk, snk, ACT.Exp).then_inc(p_ok, 1)
                    act.wait_ge(pt_ok, pair + 1)
                    nc.scalar.activation(prob_t[j], ps[:, 4:6, 0:BLK], ACT.Copy).then_inc(pt_out, 1)
                    act.wait_ge(o_ok, pair + 1)
                    nc.scalar.activation(big[:, ds(Y_T + SSD_TILES * T + pair * T, T)], ps[:, 6, 0:T],
                                         ACT.Copy).then_inc(o_out, 1)
            for q in range(4):
                act.wait_ge(mix_ok, 1)
                act.wait_ge(o_out, 8)
                a, b = q * 4 * T, (q + 1) * 4 * T
                nc.scalar.activation(sq_sb[:, a:b], y_sb[:, a:b], ACT.Square).then_inc(squared, 1)
            root(1, rs_v, rs_r)
            round_norm(1)
            with act.Fori(0, KT // 2) as i:
                for j in range(2):
                    cut_high(C_OUT + 2 * i + j + 1, (C_OUT + j + 1) % 2)
            for q in range(4):
                act.wait_ge(taken, C_OUT + 4 * (q + 1))
                a, b = q * 4 * T, (q + 1) * 4 * T
                nc.scalar.activation(sq_sb[:, a:b], h_sb[:, a:b], ACT.Square).then_inc(squared, 1)
            root(2, rs_v[:, 0:T], rs_r[:, 0:T])
            round_norm(2)
            def query_round(i, first=False):
                for j in range(2):
                    c, par = C_WQ + 2 * i + j, (C_WQ + j) % 2
                    cut_high(c + 1, 1 - par)
                    if not first:
                        act.wait_ge(score_ok, 2 * i + j - 1)
                    take(c, par, q_t[j])

            query_round(0, True)
            with act.Fori(1, PEER_HEADS) as i:
                query_round(i)

            def expert_step(c, par):
                cut_high(c + 1, 1 - par)
                if not isinstance(c, int) or c >= C_U + 2:
                    act.wait_ge(gelu_saved[par], 8 * (c - C_U - (par - C_U) % 2))
                take(c, par, gelu_out[par], ACT.Gelu)

            for j in range(2):
                expert_step(C_U + j, (C_U + j) % 2)
            with act.Fori(1, ROUTE_STEPS) as i:
                for j in range(2):
                    expert_step(C_U + 2 * i + j, (C_U + j) % 2)
            act.wait_ge(soft_in, 1)
            nc.scalar.activation(pick[2], pick[2], ACT.Exp).then_inc(soft_exp, 1)
            act.wait_ge(h_saved, 16)
            with act.Fori(0, GATE_CHUNKS // 2) as i:
                for j in range(2):
                    g = 2 * i + j
                    expert_step(C_U + 2 * ROUTE_STEPS + g, (C_U + j) % 2)
                    act.wait_ge(gate_ok, g + 1)
                    nc.scalar.activation(
                        big[:, :].rearrange("p (r t) -> p r t", t=T)[:, :, ds(g * TOK_GROUP, TOK_GROUP)],
                        ps[:, 2 + j, :].rearrange("p (t r) -> p r t", r=P), ACT.Copy).then_inc(gate_out, 1)
            first = 2 * ROUTE_STEPS + GATE_CHUNKS
            with act.Fori(0, (N_KEYS - first) // 2 - 1) as i:
                for j in range(2):
                    expert_step(C_U + first + 2 * i + j, (C_U + j) % 2)

            def round_w(e, par):
                act.wait_ge(w_ok, e + 1)
                if not (isinstance(e, int) and e < 2):
                    act.wait_ge(used, 2 * (C_V_TAB + e - 2) + 2)
                nc.scalar.activation(w_hi[:, par * T:(par + 1) * T], w_full[par], ACT.Copy).then_inc(wh_ok, 1)

            expert_step(C_V_TAB - 2, C_V_TAB % 2)
            expert_step(C_V_TAB - 1, (C_V_TAB + 1) % 2)
            round_w(0, C_V_TAB % 2)
            with act.Fori(0, N_KEYS // 2 - 1) as i:
                for j in range(2):
                    e = 1 + 2 * i + j
                    par = (C_V_TAB + 1 + j) % 2
                    cut_high(C_V_TAB + e, par)
                    round_w(e, par)
            cut_high(C_END - 1, (C_END - 1) % 2)
            round_w(N_KEYS - 1, (C_END - 1) % 2)
            for tb in range(TB):
                act.wait_ge(sum_ok, tb + 1)
                acc = ps[:, 4 * tb:4 * tb + 4, :]
                nc.scalar.activation(big[:, 8192 + tb * D:8192 + (tb + 1) * D].rearrange("p (b n) -> p b n", b=4), acc,
                                     ACT.Square, accum_out=big[:, 16384 + 8 * tb:16385 + 8 * tb]).then_inc(last_sq, 1)
            for tb in range(TB):
                act.wait_ge(last_var, tb + 1)
                s = 16384 + 8 * tb
                nc.scalar.activation(big[:, s + 2:s + 3], big[:, s + 1:s + 2], ACT.Sqrt).then_inc(last_root, 1)

        @block.vector
        def _(dve):
            own = Order(dve, dve_own)
            V = nc.vector

            def cut_low_piece(c, par, half):
                s = 2 * par + half
                dve.wait_ge(hi_done, 2 * c + half + 1)
                V.tensor_tensor(slot(low, s), slot(raw, s), slot(high, s).bitcast(F32),
                                ALU.subtract).then_inc(lo_done, 1)

            def cut_low(c, par):
                for half in range(2):
                    cut_low_piece(c, par, half)

            def newton(v, r):
                t = v
                own.step(V.reciprocal(r, r))
                own.settle()
                own.step(V.scalar_tensor_tensor(out=t, in0=r, scalar=-0.5, in1=v, op0=ALU.mult, op1=ALU.mult))
                own.settle()
                own.step(V.tensor_tensor(t, t, r, ALU.mult))
                own.settle()
                own.step(V.scalar_tensor_tensor(out=r, in0=t, scalar=1.5, in1=r, op0=ALU.add, op1=ALU.mult))
                own.settle()

            def normalise(k, v, r, sums, src, gain, rstd_of):
                dve.wait_ge(summed, k + 1)
                for bank, n, at, width in sums:
                    ins = V.tensor_scalar(v[:, at:at + n], ps[:, bank, 0:n], 1.0 / width, EPS, ALU.mult, ALU.add)
                ins.then_inc(var_ok, 1)
                dve.wait_ge(root_ok, k + 1)
                newton(v, r)
                for q in range(4):
                    for kk in range(4 * q, 4 * q + 4):
                        a, b = kk * T, (kk + 1) * T
                        ra = rstd_of(kk)
                        ins = V.scalar_tensor_tensor(out=xn_sb[:, a:b], in0=src[:, a:b], scalar=sm(gain, kk, 1),
                                                     in1=r[:, ra * T:(ra + 1) * T], op0=ALU.mult, op1=ALU.mult)
                    ins.then_inc(xn_ok, 1)
                for q in range(4):
                    a, b = q * 4 * T, (q + 1) * 4 * T
                    dve.wait_ge(xh_ok, 4 * k + q + 1)
                    V.tensor_tensor(act_lo[:, a:b], xn_sb[:, a:b], act_hi[:, a:b].bitcast(F32),
                                    ALU.subtract).then_inc(xl_ok, 1)

            dve.wait_ge(small_in, 16)
            cut_low(0, 0)
            normalise(0, rs_v[:, 0:T], rs_r[:, 0:T], [(7, T, 0, D)], x_sb, "g1", lambda kk: 0)
            V.memset(conv_in[:, :, 0:CONV_W - 1], 0.0).then_inc(pads_ok, 1)
            cut_low(1, 1)
            h16 = SSD_HEADS
            dve.wait_ge(taken, 1)
            own.step(V.tensor_scalar(dtv[0], dtv[0], sm("dt_bias")[0:h16], None, ALU.add))
            own.step(V.memset(dtv[5], 1.0))
            own.settle()
            own.step(V.tensor_scalar(dtv[1], dtv[0], -1.0, None, ALU.mult))
            own.settle()
            V.tensor_tensor(dtv[1], dtv[1], dtv[0], ALU.min).then_inc(dt_neg, 1)
            dve.wait_ge(dt_exp, 2)
            own.step(V.tensor_scalar(dtv[3], dtv[2], 2.0, None, ALU.add))
            own.settle()
            own.step(V.reciprocal(dtv[3], dtv[3]))
            own.settle()
            own.step(V.tensor_tensor(dtv[1], dtv[2], dtv[3], ALU.mult))
            own.settle()
            own.step(V.tensor_tensor(dtv[2], dtv[1], dtv[1], ALU.mult))
            own.settle()
            own.step(V.tensor_scalar(dtv[3], dtv[2], 1.0 / 17, None, ALU.mult))
            own.settle()
            for k in range(7, 0, -1):
                own.step(V.scalar_tensor_tensor(out=dtv[3], in0=dtv[3], scalar=1.0 / (2 * k + 1), in1=dtv[2],
                                                op0=ALU.add, op1=ALU.mult))
                own.settle()
            own.step(V.scalar_tensor_tensor(out=dtv[3], in0=dtv[3], scalar=1.0, in1=dtv[1],
                                            op0=ALU.add, op1=ALU.mult))
            own.step(V.tensor_scalar(dtv[0], dtv[0], 0.0, None, ALU.max))
            own.settle()
            dt = dtv[4]
            own.step(V.scalar_tensor_tensor(out=dt, in0=dtv[3], scalar=2.0, in1=dtv[0], op0=ALU.mult, op1=ALU.add))
            own.settle()
            own.step(V.tensor_scalar(dtv[3], dt, decay, -1.0, ALU.mult, ALU.mult))
            own.settle()
            own.step(V.tensor_tensor_scan(cs[:, 0:T], dtv[5], dtv[3], 0.0, ALU.mult, ALU.add))
            V.tensor_tensor_scan(cs[:, T:BLK], dtv[5][:, 0:P], dtv[3][:, P:T], 0.0, ALU.mult,
                                 ALU.add).then_inc(cs_ok, 1)

            with dve.Fori(0, CONV_TILES // 2) as i:
                own.enter(i, 3 * 2)
                for j in range(2):
                    m = 2 * i + j
                    c, par = C_CONV + 2 * i + j, (C_CONV + j) % 2
                    cut_low(c + 1, 1 - par)
                    dve.wait_ge(taken, c + 1)
                    wc, bc = _small["conv_w"][0], _small["conv_b"][0]
                    dst = big[:, ds(XBC + m * T, T)]
                    for w in range(CONV_W):
                        src = big[:, ds(CONV_IN + w + m * UP, T)]
                        tap = side[:, ds(wc + w + m * CONV_W, 1)]
                        if w == 0:
                            ins = V.tensor_scalar(dst, src, tap, side[:, ds(bc + m, 1)], ALU.mult, ALU.add)
                        else:
                            ins = V.scalar_tensor_tensor(out=dst, in0=src, scalar=tap, in1=dst,
                                                         op0=ALU.mult, op1=ALU.add)
                        if w < CONV_W - 1:
                            own.step(ins)
                            own.settle()
                    ins.then_inc(conv_ok, 1)
            own.leave(CONV_TILES // 2)
            cut_low(C_K + 1, (C_K + 1) % 2)
            cut_low(C_V + 1, (C_V + 1) % 2)
            for g in range(GROUPS):
                dve.wait_ge(cb_ok, g + 1)
                V.tensor_tensor(cb_m[g], ps[:, 2 + g, 0:BLK], sm("tri"), ALU.mult).then_inc(cbm_ok, 1)
            dve.wait_ge(small_t, 1)
            V.tensor_copy(tok_t, ps[:, 2, 0:4 * h16])
            V.tensor_copy(v_tok, ps[:, 3, 0:TB * P]).then_inc(small_t, 1)
            dve.wait_ge(small_t, 2)
            dve.wait_ge(cbm_ok, GROUPS)
            dve.wait_ge(tok_ok, 4)

            def seg(h, p):
                dve.wait_ge(bc_ok, h + 1)
                for b, (lo, hi) in enumerate(((0, T), (T, BLK))):
                    ins = V.tensor_scalar(expo[p][:, lo:hi], ps[:, 2 + p, lo:hi],
                                          big[:, ds(TAIL + 2 * BLK + 3 * T + b * h16 + h, 1)], 0.0,
                                          ALU.subtract, ALU.min)
                ins.then_inc(seg_ok, 1)

            def weigh(h, p, g):
                dve.wait_ge(exp_ok, h + 1)
                if not (isinstance(h, int) and h < 2):
                    dve.wait_ge(y_ok, h - 1)
                V.tensor_tensor(m_sb[p], expo[p], cb_m[g], ALU.mult)
                for b in range(TB):
                    ins = V.tensor_scalar(xdt[p][:, b * HEAD_DIM:(b + 1) * HEAD_DIM],
                                          big[:, ds(X_TOK + b * D_SSD + h * HEAD_DIM, HEAD_DIM)],
                                          big[:, ds(TAIL + 2 * BLK + 3 * T + (2 + b) * h16 + h, 1)], None, ALU.mult)
                ins.then_inc(m_ok, 1)

            def y_take(h, pair, p):
                dve.wait_ge(y_ok, h + 1)
                r0 = p * HEAD_DIM
                rows = slice(r0, r0 + HEAD_DIM)
                V.scalar_tensor_tensor(out=big[rows, ds(Y_T + pair * T, T)], in0=big[rows, ds(XBC + pair * T, T)],
                                       scalar=side[rows, ds(_small["d_skip"][0] + pair, 1)],
                                       in1=ps[rows, 4 + p, 0:T], op0=ALU.mult, op1=ALU.add).then_inc(y_out, 1)

            def ssd_round(i, first_of_group, g):
                for j in range(2):
                    h = 2 * i + j
                    cut_low(C_QZ + h + 1, (C_QZ + j + 1) % 2)
                    seg(h, j)
                    start = isinstance(i, int) and i == 0
                    if not (start and j == 0):
                        weigh(h - 1, 1 - j, g - 1 if first_of_group and j == 0 else g)
                    if not start:
                        y_take(h - 2, i - 1, j)

            per_group = SSD_HEADS // GROUPS // 2
            for g in range(GROUPS):
                ssd_round(g * per_group, True, g)
                if g == 0:
                    ssd_round(1, False, g)
                with dve.Fori(g * per_group + (2 if g == 0 else 1), (g + 1) * per_group) as i:
                    ssd_round(i, False, g)
            weigh(SSD_HEADS - 1, 1, GROUPS - 1)
            y_take(SSD_HEADS - 2, SSD_TILES - 1, 0)
            y_take(SSD_HEADS - 1, SSD_TILES - 1, 1)
            dve.wait_ge(z_ok, 1)
            dve.wait_ge(y_out, SSD_HEADS)
            z = view(QZ + SSD_TILES * T, SSD_TILES * T)
            V.tensor_tensor(y_sb[:, 0:SSD_TILES * T], y_sb[:, 0:SSD_TILES * T], z, ALU.mult).then_inc(mix_ok, 1)

            with dve.Fori(0, 4) as i:
                own.enter(i, 2 * 8)
                for j in range(2):
                    pair = 2 * i + j
                    mx, neg, den, snk, rec = st[j]
                    dve.wait_ge(logit_ok, pair + 1)
                    win = sm("window").rearrange("p (o m) -> p o m", o=1).broadcast_to([P, 2, BLK])
                    own.step(V.tensor_tensor(prob[j], ps[:, 2:4, 0:BLK], win, ALU.add))
                    own.settle()
                    own.step(V.tensor_reduce(mx[:, 0:2], prob[j][:, :, 0:P], AX, ALU.max))
                    own.step(V.tensor_reduce(mx[:, 2:4], prob[j][:, :, P:BLK], AX, ALU.max))
                    own.settle()
                    sink = side[:, ds(_small["sinks"][0] + pair * 2, 2)]
                    sink2 = sink.rearrange("p (o e) -> p o e", o=1).broadcast_to([P, 2, 2])
                    four = lambda t: t.rearrange("p (b e) -> p b e", e=2)
                    own.step(V.tensor_tensor(four(mx), four(mx), sink2, ALU.max))
                    own.settle()
                    own.step(V.tensor_scalar(neg, mx, -1.0, None, ALU.mult))
                    own.settle()
                    V.tensor_tensor(four(snk), four(neg), sink2, ALU.add).then_inc(max_ok, 1)
                    dve.wait_ge(p_ok, pair + 1)
                    own.step(V.tensor_tensor(den, den, snk, ALU.add))
                    own.settle()
                    own.step(V.reciprocal(rec, den))
                    own.settle()
                    for b, (lo, hi) in enumerate(((0, P), (P, BLK))):
                        part = prob[j][:, :, lo:hi]
                        ins = V.tensor_tensor(part, part, rec[:, 2 * b:2 * b + 2].rearrange(
                            "p (e o) -> p e o", o=1).broadcast_to([P, 2, hi - lo]), ALU.mult)
                        if b == 0:
                            own.step(ins)
                    ins.then_inc(pn_ok, 1)
            own.leave(4)
            half = SSD_TILES // GROUPS
            normalise(1, rs_v, rs_r, [(6, 2 * T, 0, D_SSD // GROUPS), (7, T, 2 * T, D - D_SSD)],
                      y_sb, "g_mix", lambda kk: min(kk // half, 2))
            with dve.Fori(0, KT // 2) as i:
                for j in range(2):
                    m = 2 * i + j
                    c, par = C_OUT + m, (C_OUT + j) % 2
                    cut_low(c + 1, 1 - par)
                    dve.wait_ge(used, 2 * c + 2)
                    V.tensor_tensor(big[:, ds(H_T + m * T, T)], ps[:, par, 0:T], big[:, ds(X_T + m * T, T)],
                                    ALU.add).then_inc(taken, 1)
            normalise(2, rs_v[:, 0:T], rs_r[:, 0:T], [(7, T, 0, D)], h_sb, "g2", lambda kk: 0)
            with dve.Fori(0, PEER_HEADS) as i:
                for j in range(2):
                    c, par = C_WQ + 2 * i + j, (C_WQ + j) % 2
                    cut_low(c + 1, 1 - par)
                    dve.wait_ge(score_ok, 2 * i + j + 1)
                    dst = view(SCORES, TB * 2 * PEER_HEADS * N_KEYS).rearrange("p (b m) -> p b m", b=TB)
                    V.tensor_copy(dst[:, :, ds((2 * i + j) * N_KEYS, N_KEYS)],
                                  ps[:, 2 + j, 0:TB * N_KEYS].rearrange("p (b n) -> p b n", b=TB)).then_inc(score_out, 1)
            dve.wait_ge(score_out, 2 * PEER_HEADS)
            dve.wait_ge(consts_in, 16)
            iota16 = iota[:, 0:TOPK].rearrange("p (o a) -> p o a", o=1).broadcast_to([P, TOPK, TOPK])

            def best(src, spare, vals, idx, k):
                if k == 0:
                    own.step(V.max(vals[:, 0:8], src))
                elif k == 1:
                    own.step(V.max_index(idx[:, 0:8], vals[:, 0:8], src))
                    own.step(V.match_replace(spare, vals[:, 0:8], src, LOWEST))
                elif k == 2:
                    own.step(V.max(vals[:, 8:16], spare))
                else:
                    own.step(V.max_index(idx[:, 8:16], vals[:, 8:16], spare))

            def met():
                V.memset(r_mark, 0.0)

            PER = 27
            with dve.Fori(0, ROUTE_STEPS) as i:
                own.enter(i, PER)
                c = C_U + 2 * i
                own.step(V.tensor_copy(r_s.rearrange("p s n -> p (s n)"), big[:, ds(SCORES + i * 2 * N_KEYS, 2 * N_KEYS)]))
                own.settle()
                for k in range(4):
                    met()
                    for s in range(2):
                        best(r_s[:, s], r_s2[:, s], r_v[:, s * TOPK:(s + 1) * TOPK], r_ix[:, s * TOPK:(s + 1) * TOPK], k)
                    own.settle()
                    if k == 1:
                        cut_low_piece(c + 1, (C_U + 1) % 2, 0)
                cut_low_piece(c + 1, (C_U + 1) % 2, 1)
                own.step(V.tensor_copy(r_ixf, r_ix))
                va = r_v[:, 0:TOPK].rearrange("p (a o) -> p a o", o=1).broadcast_to([P, TOPK, TOPK])
                vb = r_v[:, TOPK:2 * TOPK].rearrange("p (o b) -> p o b", o=1).broadcast_to([P, TOPK, TOPK])
                own.step(V.tensor_tensor(r_c.rearrange("p (a b) -> p a b", a=TOPK), va, vb, ALU.add))
                own.settle()
                for k in range(4):
                    met()
                    best(r_c, r_c2, r_tv, r_tp, k)
                    own.settle()
                cut_low_piece(c + 2, C_U % 2, 0)
                own.step(V.tensor_scalar(r_ab[0], r_tp, 4, None, ALU.logical_shift_right))
                own.step(V.tensor_scalar(r_ab[1], r_tp, TOPK - 1, None, ALU.bitwise_and))
                own.step(V.tensor_copy(big[:, ds(PICKS + 512 + i * TOPK, TOPK)], r_tv))
                own.settle()
                for s in range(2):
                    own.step(V.tensor_tensor(r_eq[s], iota16, r_ab[s].rearrange("p (k o) -> p k o", o=1).broadcast_to(
                        [P, TOPK, TOPK]), ALU.is_equal))
                own.settle()
                for s in range(2):
                    own.step(V.tensor_tensor(r_eq[s], r_eq[s], r_ixf[:, s * TOPK:(s + 1) * TOPK].rearrange(
                        "p (o a) -> p o a", o=1).broadcast_to([P, TOPK, TOPK]), ALU.mult))
                own.settle()
                for s in range(2):
                    own.step(V.tensor_reduce(big[:, ds(PICKS + s * 256 + i * TOPK, TOPK)], r_eq[s], AX, ALU.add))
                cut_low_piece(c + 2, C_U % 2, 1)
                own.settle()
            own.leave(ROUTE_STEPS)
            by_pick = lambda t: t.rearrange("p (s k) -> p s k", k=TOPK)
            gates = by_pick(pick[2])
            wide = lambda t: t.broadcast_to([P, ROUTE_STEPS, TOPK])
            own.step(V.tensor_copy(r_sum, gates[:, :, 0:1].rearrange("p s k -> p (s k)")))
            own.settle()
            V.tensor_tensor(gates, gates, wide(r_sum.rearrange("p (s o) -> p s o", o=1)), ALU.subtract).then_inc(soft_in, 1)
            dve.wait_ge(soft_exp, 1)
            own.step(V.tensor_reduce(r_sum, gates, AX, ALU.add))
            own.settle()
            own.step(V.reciprocal(r_sum, r_sum))
            own.settle()
            V.tensor_tensor(gates, gates, wide(r_sum.rearrange("p (s o) -> p s o", o=1)), ALU.mult).then_inc(picks_ok, 1)
            dve.wait_ge(picks_tr, 1)
            for tb in range(TB):
                own.step(V.tensor_copy(pick_t[:, :].rearrange("p (a t) -> p a t", a=3)[:, :, tb * P:(tb + 1) * P],
                                       ps[:, 4 + tb, 0:3 * P].rearrange("p (a t) -> p a t", a=3)))
            own.settle()
            def spread_round(i, first=False):
                for j in range(2):
                    g = 2 * i + j
                    cut_low(C_U + 2 * ROUTE_STEPS + g + 1, (C_U + j + 1) % 2)
                    if not (first and j == 0):
                        dve.wait_ge(gate_ok, g)
                    for t in range(TOK_GROUP):
                        at = g * TOK_GROUP + t
                        V.tensor_scalar(hot_col[:, t * P:(t + 1) * P], iota, pick_t[:, ds(at + T, 1)], None, ALU.is_equal)
                        ins = V.tensor_scalar(hot_row[:, t * P:(t + 1) * P], iota, pick_t[:, ds(at, 1)],
                                              pick_t[:, ds(at + 2 * T, 1)], ALU.is_equal, ALU.mult)
                    ins.then_inc(hot_ok, 1)

            spread_round(0, True)
            with dve.Fori(1, GATE_CHUNKS // 2) as i:
                spread_round(i)
            first = 2 * ROUTE_STEPS + GATE_CHUNKS
            with dve.Fori(0, (N_KEYS - first) // 2 - 1) as i:
                for j in range(2):
                    cut_low(C_U + first + 2 * i + j + 1, (C_U + j + 1) % 2)

            def weights(e, par, between):
                dve.wait_ge(gelu_back[par], 8 * (e + 2 - (par - C_V_TAB) % 2))
                own_gate = big[:, ds(e * T, T)]
                V.tensor_tensor(w_full[par], own_gate, gelu_in[par], ALU.mult).then_inc(w_ok, 1)
                between()
                dve.wait_ge(wh_ok, e + 1)
                V.tensor_tensor(w_lo[:, par * T:(par + 1) * T], w_full[par], w_hi[:, par * T:(par + 1) * T].bitcast(F32),
                                ALU.subtract).then_inc(wl_ok, 1)

            cut_low(C_V_TAB - 1, (C_V_TAB + 1) % 2)
            cut_low(C_V_TAB, C_V_TAB % 2)
            dve.wait_ge(gate_out, GATE_CHUNKS)
            weights(0, C_V_TAB % 2, lambda: None)

            def v_step(e, par):
                cut_low_piece(C_V_TAB + e, par, 0)
                weights(e, par, lambda: cut_low_piece(C_V_TAB + e, par, 1))

            with dve.Fori(0, N_KEYS // 2 - 1) as i:
                for j in range(2):
                    v_step(1 + 2 * i + j, (C_V_TAB + 1 + j) % 2)
            v_step(N_KEYS - 1, (C_END - 1) % 2)
            dve.wait_ge(gf_in, 16)
            for tb in range(TB):
                s = 16384 + 8 * tb
                dve.wait_ge(last_sq, tb + 1)
                V.tensor_scalar(big[:, s + 1:s + 2], big[:, s:s + 1], 1.0 / D, EPS, ALU.mult, ALU.add).then_inc(last_var, 1)
            for tb in range(TB):
                s = 16384 + 8 * tb
                dve.wait_ge(last_root, tb + 1)
                newton(big[:, s + 1:s + 2], big[:, s + 2:s + 3])
                for q in range(2):
                    n = D // 2
                    V.scalar_tensor_tensor(
                        out=big[:, (2 * tb + q) * n:(2 * tb + q + 1) * n].rearrange("p (b n) -> p b n", b=2),
                        in0=ps[:, 4 * tb + 2 * q:4 * tb + 2 * q + 2, :], scalar=big[:, s + 2:s + 3],
                        in1=g_last[:, q * n:(q + 1) * n].rearrange("p (b n) -> p b n", b=2),
                        op0=ALU.mult, op1=ALU.mult).then_inc(last_ok, 1)

        @block.tensor
        def _(pe):
            mm = nc.tensor.matmul

            def product(c, par):
                if not (isinstance(c, int) and c < 2):
                    pe.wait_ge(taken, c - 1)
                acc = ps[:, par, 0:T]
                for half in range(2):
                    s = 2 * par + half
                    pe.wait_ge(lo_done, 2 * c + half + 1)
                    for k in range(8):
                        kk = 8 * half + k
                        a_hi, a_lo = act_hi[:, kk * T:(kk + 1) * T], act_lo[:, kk * T:(kk + 1) * T]
                        wh = high[:, s * PIECE + k * P:s * PIECE + (k + 1) * P]
                        wl = low[:, s * PIECE + k * P:s * PIECE + (k + 1) * P]
                        mm(acc, wh, a_hi, start=(kk == 0), stop=False)
                        mm(acc, wh, a_lo, start=False, stop=False)
                        ins = mm(acc, wl, a_hi, start=False, stop=(kk == KT - 1))
                    ins.then_inc(used, 1)

            def sum_squares(k, parts):
                for bank, lo, tiles in parts:
                    for n, t in enumerate(tiles):
                        if n % 4 == 0:
                            pe.wait_ge(squared, 4 * k + t // 4 + 1)
                        ins = mm(ps[:, bank, lo:lo + T], sm("ones"), sq_sb[:, t * T:(t + 1) * T],
                                 start=(n == 0), stop=(n == len(tiles) - 1))
                ins.then_inc(summed, 1)

            pe.wait_ge(small_in, 16)
            sum_squares(0, [(7, 0, range(KT))])
            pe.wait_ge(xl_ok, 4)
            for c in range(3):
                product(c, c % 2)
            with pe.Fori(0, (C_QZ - 3) // 2) as i:
                for j in range(2):
                    product(3 + 2 * i + j, (3 + j) % 2)
            pe.wait_ge(silu_ok, 1)
            tile = lambda n: view(XBC + n * T, T)
            for g in range(GROUPS):
                b_t, c_t = tile(SSD_TILES + g), tile(SSD_TILES + GROUPS + g)
                mm(ps[:, 2 + g, 0:T], b_t[:, 0:P], c_t, start=True, stop=True)
                mm(ps[:, 2 + g, T:BLK], b_t[:, P:T], c_t[:, P:T], start=True, stop=True).then_inc(cb_ok, 1)
            pe.wait_ge(silu_ok, 2)
            pe.wait_ge(consts_in, 16)
            for b in range(4):
                for n in range(4):
                    tb, ch = (4 * b + n) // SSD_TILES, (4 * b + n) % SSD_TILES
                    ins = nc.tensor.transpose(ps[:, 4 + b, n * P:(n + 1) * P], tile(ch)[:, tb * P:(tb + 1) * P], ident)
                ins.then_inc(tr_ok, 1)
            pe.wait_ge(cs_ok, 1)
            pe.wait_ge(cbm_ok, GROUPS)
            h16 = SSD_HEADS
            for n, rows in enumerate((cs[:, 0:P], cs[:, T:BLK], dtv[4][:, 0:P], dtv[4][:, P:T])):
                nc.tensor.transpose(ps[:, 2, n * h16:(n + 1) * h16], rows, ident[0:h16, 0:h16])
            pe.wait_ge(taken, C_V + 1)
            for tb in range(TB):
                ins = nc.tensor.transpose(ps[:, 3, tb * P:(tb + 1) * P], v_t[:, tb * P:(tb + 1) * P], ident)
            ins.then_inc(small_t, 1)
            pe.wait_ge(rows_ok, 1)
            pe.wait_ge(small_t, 2)
            pe.wait_ge(tok_ok, 4)

            def spread(h, p):
                if not (isinstance(h, int) and h < 2):
                    pe.wait_ge(seg_ok, h - 1)
                mm(ps[:, 2 + p, 0:BLK], sm("ones")[0:h16, :], cs_rows_at(h), start=True, stop=True).then_inc(bc_ok, 1)

            def cs_rows_at(h):
                return big[0:h16, ds(SQ + h * BLK, BLK)]

            def y_of(h, p):
                pe.wait_ge(m_ok, h + 1)
                if not (isinstance(h, int) and h < 2):
                    pe.wait_ge(y_out, h - 1)
                dst = ps[p * HEAD_DIM:(p + 1) * HEAD_DIM, 4 + p, 0:T]
                mm(dst, xdt[p][:, 0:HEAD_DIM], m_sb[p][:, 0:T], start=True, stop=True)
                mm(dst[:, P:T], xdt[p][:, HEAD_DIM:P], m_sb[p][:, T:BLK], start=False, stop=True,
                   skip_group_check=True).then_inc(y_ok, 1)

            def ssd_round(i):
                for j in range(2):
                    h = 2 * i + j
                    spread(h, j)
                    product(C_QZ + h, (C_QZ + j) % 2)
                    if not (isinstance(i, int) and i == 0 and j == 0):
                        y_of(h - 1, 1 - j)

            ssd_round(0)
            ssd_round(1)
            with pe.Fori(2, SSD_HEADS // 2) as i:
                ssd_round(i)
            y_of(SSD_HEADS - 1, 1)

            with pe.Fori(0, 4) as i:
                for j in range(2):
                    pair = 2 * i + j
                    pe.wait_ge(q_ok, pair + 1)
                    for e in range(2):
                        rows = slice(e * HEAD_DIM, (e + 1) * HEAD_DIM)
                        q, kk = q_in[j][rows], k_t[rows]
                        mm(ps[:, 2 + e, 0:P], q[:, 0:P], kk[:, 0:P], start=True, stop=True)
                        ins = mm(ps[:, 2 + e, P:BLK], q[:, P:T], kk, start=True, stop=True)
                    ins.then_inc(logit_ok, 1)
                    pe.wait_ge(pn_ok, pair + 1)
                    for e in range(2):
                        for m in range(3):
                            ins = nc.tensor.transpose(ps[:, 4 + e, m * P:(m + 1) * P],
                                                      prob[j][:, e, m * P:(m + 1) * P], ident)
                    ins.then_inc(pt_ok, 1)
                    pe.wait_ge(pt_out, pair + 1)
                    for e in range(2):
                        dst = ps[e * HEAD_DIM:(e + 1) * HEAD_DIM, 6, :]
                        v = [v_tok[:, b * P + e * HEAD_DIM:b * P + (e + 1) * HEAD_DIM] for b in range(TB)]
                        pt = prob_t[j][:, e]
                        mm(dst[:, 0:P], v[0], pt[:, 0:P], start=True, stop=True)
                        mm(dst[:, P:T], v[0], pt[:, P:T], start=True, stop=False)
                        ins = mm(dst[:, P:T], v[1], pt[:, T:BLK], start=False, stop=True)
                    ins.then_inc(o_ok, 1)
            pe.wait_ge(o_out, 8)
            half = SSD_TILES // GROUPS
            sum_squares(1, [(6, 0, range(half)), (6, T, range(half, 2 * half)), (7, 0, range(2 * half, KT))])
            pe.wait_ge(xl_ok, 8)
            with pe.Fori(0, KT // 2) as i:
                for j in range(2):
                    product(C_OUT + 2 * i + j, (C_OUT + j) % 2)
            sum_squares(2, [(7, 0, range(KT))])
            pe.wait_ge(xl_ok, 12)
            pe.wait_ge(keys_in, 16)

            def scores(m, j):
                pe.wait_ge(taken, C_WQ + 1 + m)
                if not (isinstance(m, int) and m < 2):
                    pe.wait_ge(score_out, m - 1)
                for tb in range(TB):
                    ins = mm(ps[:, 2 + j, tb * N_KEYS:(tb + 1) * N_KEYS], q_t[j][:, tb * P:(tb + 1) * P],
                             big[:, ds(CONV_IN + m * N_KEYS, N_KEYS)], start=True, stop=True)
                ins.then_inc(score_ok, 1)

            product(C_WQ, C_WQ % 2)
            for j in range(2):
                product(C_WQ + 1 + j, (C_WQ + 1 + j) % 2)
                scores(j, j)
            with pe.Fori(1, PEER_HEADS - 1) as i:
                for j in range(2):
                    product(C_WQ + 1 + 2 * i + j, (C_WQ + 1 + j) % 2)
                    scores(2 * i + j, j)
            product(C_U - 1, (C_U - 1) % 2)
            scores(2 * PEER_HEADS - 2, 0)
            scores(2 * PEER_HEADS - 1, 1)
            with pe.Fori(0, ROUTE_STEPS) as i:
                for j in range(2):
                    product(C_U + 2 * i + j, (C_U + j) % 2)
            pe.wait_ge(picks_ok, 1)
            for tb in range(TB):
                for a in range(3):
                    ins = nc.tensor.transpose(ps[:, 4 + tb, a * P:(a + 1) * P], pick[a][:, tb * P:(tb + 1) * P], ident)
            ins.then_inc(picks_tr, 1)
            def gate_round(i, first=False):
                for j in range(2):
                    g = 2 * i + j
                    product(C_U + 2 * ROUTE_STEPS + g, (C_U + j) % 2)
                    pe.wait_ge(hot_ok, g + 1)
                    if not first:
                        pe.wait_ge(gate_out, g - 1)
                    for t in range(TOK_GROUP):
                        ins = mm(ps[:, 2 + j, t * P:(t + 1) * P], hot_col[:, t * P:(t + 1) * P],
                                 hot_row[:, t * P:(t + 1) * P], start=True, stop=True)
                    ins.then_inc(gate_ok, 1)

            gate_round(0, True)
            with pe.Fori(1, GATE_CHUNKS // 2) as i:
                gate_round(i)
            first = 2 * ROUTE_STEPS + GATE_CHUNKS
            with pe.Fori(0, (N_KEYS - first) // 2) as i:
                for j in range(2):
                    product(C_U + first + 2 * i + j, (C_U + j) % 2)
            pe.wait_ge(taken, C_V_TAB)
            pe.wait_ge(gate_out, GATE_CHUNKS)

            def expert_rows(e, par, start=False, stop=False):
                c = C_V_TAB + e
                pe.wait_ge(wl_ok, e + 1)
                for hf in range(2):
                    s = 2 * par + hf
                    pe.wait_ge(lo_done, 2 * c + hf + 1)
                    for tb in range(TB):
                        at = par * T + tb * P
                        wh, wl = w_hi[:, at:at + P], w_lo[:, at:at + P]
                        vh = [high[:, s * PIECE + n * 512:s * PIECE + (n + 1) * 512] for n in range(2)]
                        vl = [low[:, s * PIECE + n * 512:s * PIECE + (n + 1) * 512] for n in range(2)]
                        acc = [ps[:, 4 * tb + 2 * hf + n, :] for n in range(2)]
                        for n in range(2):
                            mm(acc[n], wh, vh[n], start=start, stop=False, skip_group_check=True)
                        for n in range(2):
                            mm(acc[n], wh, vl[n], start=False, stop=False, skip_group_check=True)
                        for n in range(2):
                            ins = mm(acc[n], wl, vh[n], start=False, stop=stop, skip_group_check=True)
                    ins.then_inc(used, 1)

            for j in range(2):
                expert_rows(j, (C_V_TAB + j) % 2, start=(j == 0))
            with pe.Fori(1, N_KEYS // 2 - 1) as i:
                for j in range(2):
                    expert_rows(2 * i + j, (C_V_TAB + j) % 2)
            for e in range(N_KEYS - 2, N_KEYS):
                expert_rows(e, (C_V_TAB + e) % 2, stop=(e == N_KEYS - 1))
            pe.wait_ge(h_in, 16)
            for tb in range(TB):
                for k in range(KT):
                    ins = mm(ps[:, 4 * tb + k // 4, (k % 4) * P:(k % 4 + 1) * P],
                             h_back[:, k * T + tb * P:k * T + (tb + 1) * P], ident, start=False, stop=True,
                             skip_group_check=True)
                ins.then_inc(sum_ok, 1)


def kernel(x, norm1_g, w_in, conv_w, conv_b, dt_bias, a_log, d_skip, ssd_norm_g, attn_sinks, attn_norm_g,
           w_out, norm2_g, peer_wq, peer_keys, peer_u, peer_v, norm_f_g):
    import numpy as np
    import concourse.bacc as bacc
    from concourse.bass_utils import run_bass_kernel_spmd

    f32 = np.float32
    arr = lambda a: np.asarray(a)
    conv_dim = CONV_TILES * P
    kv = 2 * HEAD_DIM
    o_z, o_xbc = 0, D_SSD
    o_dt = o_xbc + conv_dim
    o_q = o_dt + SSD_HEADS
    o_k = o_q + D - D_SSD
    o_v = o_k + kv
    heads = np.arange(SSD_HEADS).reshape(2, SSD_TILES).T.ravel()
    att = (heads[:, None] * HEAD_DIM + np.arange(HEAD_DIM)).ravel()

    def chunks(w):
        return np.ascontiguousarray(w.reshape(KT, P, -1, P).transpose(2, 1, 0, 3)).reshape(-1, P, D)

    wi = arr(w_in)[0]
    dt_cols = np.zeros((D, P), f32)
    dt_cols[:, :SSD_HEADS] = wi[:, o_dt:o_q]
    wi = np.concatenate([dt_cols, wi[:, o_xbc:o_dt], wi[:, o_k:o_v], wi[:, o_v:o_v + kv], wi[:, o_q + att],
                         wi[:, o_z:o_xbc]], axis=1)
    wo = arr(w_out)[0]
    wo = np.concatenate([wo[:D_SSD], wo[D_SSD + att]], axis=0)
    cols = lambda a: arr(a).reshape(-1, P).T

    def column(a):
        c = np.zeros((P, 1), f32)
        c[:SSD_HEADS, 0] = arr(a)[0]
        return c

    pos = np.arange(P)
    causal = (pos[:, None] <= pos[None, :]).astype(f32)
    tri = np.concatenate([causal, np.ones((P, P), f32), causal], axis=1)
    chunk = 64
    qc, kc = pos[:, None] // chunk, np.arange(T)[None, :] // chunk
    seen = np.concatenate([(kc[:, :P] <= qc) & (kc[:, :P] >= qc - 1),
                           (kc <= qc + 2) & (kc >= qc + 1)], axis=1)
    window = np.where(seen, f32(0), f32(-1e30)).astype(f32)
    parts = {
        "ones": np.ones((P, P), f32), "tri": tri, "window": window,
        "g1": cols(norm1_g), "g_mix": np.concatenate([cols(ssd_norm_g), arr(attn_norm_g)[0][att].reshape(-1, P).T], axis=1),
        "g2": cols(norm2_g), "d_skip": np.repeat(arr(d_skip)[0], HEAD_DIM).reshape(-1, P).T,
        "conv_w": arr(conv_w)[0].reshape(CONV_W, CONV_TILES, P).transpose(2, 1, 0).reshape(P, -1),
        "conv_b": cols(conv_b), "dt_bias": column(dt_bias), "a_log": column(a_log),
        "sinks": np.broadcast_to(arr(attn_sinks)[0][heads], (P, 2 * SSD_TILES)),
    }
    arrays = {
        "x_t": arr(x)[0].T.reshape(KT, P, T).transpose(1, 0, 2).reshape(P, KT * T),
        "small": np.concatenate([parts[n] for n in _small], axis=1),
        "id_iota": np.concatenate([np.eye(P, dtype=f32), np.broadcast_to(pos.astype(f32), (P, P))], axis=1),
        "w_in": chunks(wi),
        "w_out": chunks(wo),
        "w_q": chunks(arr(peer_wq)[0]),
        "keys": arr(peer_keys)[0].reshape(2 * PEER_HEADS, N_KEYS, P).transpose(2, 0, 1).reshape(P, -1),
        "u_tab": np.ascontiguousarray(arr(peer_u)[0].reshape(N_KEYS, P, KT, P).transpose(0, 3, 2, 1)).reshape(N_KEYS, P, D),
        "v_tab": arr(peer_v)[0].reshape(N_KEYS, P, D),
        "g_f": np.broadcast_to(arr(norm_f_g), (P, D)),
    }
    nc = bacc.Bacc("TRN2", target_bir_lowering=False, num_devices=1, dynamic_dma_scratch_size=4096)
    args = []
    for name in arrays:
        arrays[name] = np.ascontiguousarray(arrays[name])
        args.append(nc.dram_tensor(name, arrays[name].shape, F32, kind="ExternalInput").ap())
    args.append(nc.dram_tensor("out", (T, D), F32, kind="ExternalOutput").ap())
    build(nc, *args)
    r = run_bass_kernel_spmd(nc, [arrays], core_ids=[0])
    return r.results[0]["out"].reshape(1, T, D)
```

```python
from contextlib import ExitStack

import concourse.bass as bass
from concourse import mybir

F32 = mybir.dt.float32
F32R = mybir.dt.float32r
U32 = mybir.dt.uint32
ALU = mybir.AluOpType
ACT = mybir.ActivationFunctionType
AX = mybir.AxisListType.X
ds = bass.ds

P = 128
T = 256
D = 2048
KT = D // P
TB = T // P
SSD_HEADS, HEAD_DIM, GROUPS = 16, 64, 2
D_SSD = SSD_HEADS * HEAD_DIM
SSD_TILES = D_SSD // P
CONV_W = 4
CONV_TILES = SSD_TILES + 2 * GROUPS
PEER_HEADS, TOPK, N_KEYS = 8, 16, 128
EPS = 1e-6
LOWEST = -3.0e38
BLK = T + P

N_IN = 1 + CONV_TILES + 2 + 2 * SSD_TILES
C_DT, C_CONV, C_K, C_V, C_Q = 0, 1, 1 + CONV_TILES, 2 + CONV_TILES, 3 + CONV_TILES
C_Z = C_Q + SSD_TILES
C_OUT = N_IN
C_WQ = C_OUT + KT
C_U = C_WQ + 2 * PEER_HEADS
C_V_TAB = C_U + N_KEYS
C_END = C_V_TAB + N_KEYS
ROUTE_STEPS = TB * PEER_HEADS
ROUTE_SPAN = 3
ROUTE_CHUNKS = ROUTE_SPAN * ROUTE_STEPS
TOK_GROUP = 4
GATE_CHUNKS = T // TOK_GROUP
PIECE = 1024
H_PARTS = 4
RING = 4
X_T, H_T, Y_T, SQ, XN = (k * KT * T for k in range(5))

_small = {}
_at = 0
for _name, _n in (("ones", P), ("tri", BLK), ("window", BLK), ("g1", KT), ("g_mix", KT), ("g2", KT),
                  ("d_skip", SSD_TILES), ("conv_w", CONV_TILES * CONV_W), ("conv_b", CONV_TILES),
                  ("dt_bias", 1), ("a_log", 1), ("sinks", 2 * SSD_TILES)):
    _small[_name] = (_at, _n)
    _at += _n
SMALL = _at


class Order:

    def __init__(self, eng, sem):
        self.eng, self.sem, self.n, self.here = eng, sem, 0, 0

    def step(self, ins):
        ins.then_inc(self.sem, 1)
        self.n = self.n + 1
        self.here += 1

    def settle(self):
        self.eng.wait_ge(self.sem, self.n)

    def enter(self, i, per):
        self.base, self.per, self.here = self.n, per, 0
        self.n = self.base + i * per

    def leave(self, rounds):
        assert self.here == self.per, (self.here, self.per)
        self.n = self.base + rounds * self.per


def build(nc, x_t, small, id_iota, w_in, w_out, w_q, keys, u_tab, v_tab, g_f, out):
    h_scratch = nc.dram_tensor("h_scratch", (P, KT * T), F32).ap()
    gelu_scratch = nc.dram_tensor("gelu_scratch", (N_KEYS, P, T), F32).ap()

    with ExitStack() as ctx:
        def sb(stack, name, cols, dt=F32):
            return stack.enter_context(nc.sbuf_tensor(name, [P, cols], dt))

        def sem(name):
            return ctx.enter_context(nc.semaphore(name))

        raw = sb(ctx, "raw", RING * PIECE)
        high = sb(ctx, "high", RING * PIECE, F32R)
        low = sb(ctx, "low", RING * PIECE, F32R)
        with ExitStack() as front:
            sb(front, "front_part", SQ)
            act2_hi = sb(front, "act2_hi", KT * T, F32R)
            act2_lo = sb(front, "act2_lo", KT * T, F32R)
        big = sb(ctx, "big", N_KEYS * T)
        side = sb(ctx, "side", 1536)
        consts = sb(ctx, "consts", 2 * P)
        ident, iota = consts[:, 0:P], consts[:, P:2 * P]
        with ExitStack() as early:
            act_hi = sb(early, "act_hi", KT * T, F32R)
            act_lo = sb(early, "act_lo", KT * T, F32R)
            pick_t = sb(early, "pick_t", 3 * T)
        h_back = sb(ctx, "h_back", KT * T)
        g_last = sb(ctx, "g_last", D)
        sb(ctx, "unused", KT * T - D)
        w_hi = sb(ctx, "w_hi", 2 * T, F32R)
        w_lo = sb(ctx, "w_lo", 2 * T, F32R)
        ps = ctx.enter_context(nc.psum_tensor("ps", [P, 8, 512], F32))

        def view(at, cols):
            return big[:, at:at + cols]

        x_sb, h_sb, y_sb, sq_sb, xn_sb = (view(a, KT * T) for a in (X_T, H_T, Y_T, SQ, XN))
        UP = CONV_W - 1 + T + 1
        CONV_IN, XBC = 20480, 20480 + CONV_TILES * UP
        QZ = XBC + CONV_TILES * T
        conv_in = view(CONV_IN, CONV_TILES * UP).rearrange("p (c u) -> p c u", u=UP)
        X_TOK = H_T
        x_tok = view(X_TOK, TB * D_SSD)
        E_AT = H_T + TB * D_SSD
        expo = [view(E_AT + k * BLK, BLK) for k in range(2)]
        m_sb = [view(E_AT + (2 + k) * BLK, BLK) for k in range(2)]
        xdt = [view(E_AT + 4 * BLK + k * P, P) for k in range(2)]
        TAIL = QZ + KT * T
        cb_m = [view(TAIL + g * BLK, BLK) for g in range(GROUPS)]
        k_t = view(TAIL + 2 * BLK, T)
        v_t = view(TAIL + 2 * BLK + T, T)
        v_tok = view(TAIL + 2 * BLK + 2 * T, TB * P)
        tok_t = view(TAIL + 2 * BLK + 3 * T, 4 * SSD_HEADS)
        assert TAIL + 2 * BLK + 4 * T + 4 * SSD_HEADS <= N_KEYS * T
        cs_rows = view(SQ, SSD_HEADS * BLK)
        DT = SQ + SSD_HEADS * BLK
        dtv = [big[0:SSD_HEADS, DT + k * T:DT + (k + 1) * T] for k in range(6)]
        cs = big[0:SSD_HEADS, DT + 6 * T:DT + 6 * T + BLK]
        decay = big[0:SSD_HEADS, DT + 6 * T + BLK:DT + 6 * T + BLK + 1]
        assert 6 * T + BLK + 1 <= 2048
        q_in = [view(SQ + k * T, T) for k in range(2)]
        A2 = SQ + 2 * T
        prob = [view(A2 + k * 2 * BLK, 2 * BLK).rearrange("p (e m) -> p e m", e=2) for k in range(2)]
        A3 = A2 + 4 * BLK
        prob_t = [view(A3 + k * 2 * BLK, 2 * BLK).rearrange("p (e m) -> p e m", e=2) for k in range(2)]
        A4 = A3 + 4 * BLK
        st = [[view(A4 + (k * 5 + m) * 4, 4) for m in range(5)] for k in range(2)]
        key_t = view(CONV_IN, 2 * PEER_HEADS * N_KEYS)
        SCORES = QZ
        q_t = [view(XBC + k * T, T) for k in range(2)]
        r_s, r_s2 = (view(k * 256, 256).rearrange("p (s n) -> p s n", s=2) for k in range(2))
        r_c, r_c2 = (view(512 + k * 256, 256) for k in range(2))
        r_eq = [view(1024 + k * 256, 256).rearrange("p (k a) -> p k a", a=TOPK) for k in range(2)]
        r_v = view(1536, 2 * TOPK)
        r_ix = view(1568, 2 * TOPK).bitcast(U32)
        r_ixf = view(1600, 2 * TOPK)
        r_tv = view(1632, TOPK)
        r_tp = view(1648, TOPK).bitcast(U32)
        r_ab = [view(1664 + k * TOPK, TOPK).bitcast(U32) for k in range(2)]
        PICKS = 2048
        pick = [view(PICKS + k * 256, 256) for k in range(3)]
        r_sum = view(2816, ROUTE_STEPS)
        r_mark = view(2816 + ROUTE_STEPS, 1)
        rs_v, rs_r = (view(XBC + (2 + 3 * k) * T, 3 * T) for k in range(2))
        h_sq = [view(XBC + (8 + k) * T, T) for k in range(2)]
        h_sum = view(XBC + 10 * T, T)
        rstd1 = view(TAIL + 2 * BLK + 3 * T + 4 * SSD_HEADS, T)

        def sm(name, lo=0, n=None):
            at, size = _small[name]
            return side[:, at + lo:at + lo + (size if n is None else n)]

        gelu_out = [side[:, k * T:(k + 1) * T] for k in range(2)]
        hot_col = side[:, 2 * T:2 * T + TOK_GROUP * P]
        hot_row = side[:, 4 * T:4 * T + TOK_GROUP * P]
        gelu_in = [side[:, (2 + k) * T:(3 + k) * T] for k in range(2)]
        w_full = [side[:, (4 + k) * T:(5 + k) * T] for k in range(2)]

        small_in = sem("small_in")
        consts_in = sem("consts_in")
        x_in = [sem(f"x_in{k}") for k in range(4)]
        keys_in = sem("keys_in")
        raw_in = [sem(f"raw_in{k}") for k in range(RING)]
        hi_done = sem("hi_done")
        lo_done = sem("lo_done")
        used = sem("used")
        taken = sem("taken")
        squared = sem("squared")
        summed = sem("summed")
        var_ok = sem("var_ok")
        root_ok = sem("root_ok")
        xn_ok = sem("xn_ok")
        xh_ok = sem("xh_ok")
        xl_ok = sem("xl_ok")
        tile_ok = sem("tile_ok")
        tile_hi = sem("tile_hi")
        tile_lo = sem("tile_lo")
        h_summed = sem("h_summed")
        h_squared = sem("h_squared")
        x_summed = sem("x_summed")
        dve_own = sem("dve_own")
        pads_ok = sem("pads_ok")
        conv_ok = sem("conv_ok")
        silu_ok = sem("silu_ok")
        dt_neg = sem("dt_neg")
        dt_exp = sem("dt_exp")
        cs_ok = sem("cs_ok")
        rows_ok = sem("rows_ok")
        tr_ok = sem("tr_ok")
        tok_ok = sem("tok_ok")
        cb_ok = sem("cb_ok")
        cbm_ok = sem("cbm_ok")
        small_t = sem("small_t")
        bc_ok = sem("bc_ok")
        seg_ok = sem("seg_ok")
        exp_ok = sem("exp_ok")
        m_ok = sem("m_ok")
        y_ok = sem("y_ok")
        y_out = sem("y_out")
        z_ok = sem("z_ok")
        q_ok = sem("q_ok")
        logit_ok = sem("logit_ok")
        max_ok = sem("max_ok")
        p_ok = sem("p_ok")
        pn_ok = sem("pn_ok")
        pt_ok = sem("pt_ok")
        pt_out = sem("pt_out")
        o_ok = sem("o_ok")
        o_out = sem("o_out")
        mix_ok = sem("mix_ok")
        score_ok = sem("score_ok")
        score_out = sem("score_out")
        h_saved = sem("h_saved")
        soft_in = sem("soft_in")
        soft_exp = sem("soft_exp")
        picks_ok = sem("picks_ok")
        picks_tr = sem("picks_tr")
        hot_ok = sem("hot_ok")
        gate_ok = sem("gate_ok")
        gate_out = sem("gate_out")
        gelu_saved = [sem(f"gelu_saved{k}") for k in range(2)]
        gelu_back = [sem(f"gelu_back{k}") for k in range(2)]
        w_ok = sem("w_ok")
        wh_ok = sem("wh_ok")
        wl_ok = sem("wl_ok")
        h_in = sem("h_in")
        gf_in = sem("gf_in")
        sum_ok = sem("sum_ok")
        last_sq = sem("last_sq")
        last_var = sem("last_var")
        last_root = sem("last_root")
        last_ok = sem("last_ok")
        stored = sem("stored")

        def slot(t, s):
            return t[:, s * PIECE:(s + 1) * PIECE]

        block = ctx.enter_context(nc.Block())

        @block.sync
        def _(sp):
            def load(c, par, src):
                for half in range(2):
                    s = 2 * par + half
                    if not (isinstance(c, int) and c < 2):
                        sp.wait_ge(lo_done, 2 * c + half - 3)
                    sp.dma_start(slot(raw, s), src[:, half * PIECE:(half + 1) * PIECE]).then_inc(raw_in[s], 16)

            def load_all(tab, first, count, extra=None):
                with sp.Fori(0, count // 2) as i:
                    for j in range(2):
                        load(first + 2 * i + j, (first + j) % 2, tab[2 * i + j])
                        if extra:
                            extra(2 * i + j, (first + j) % 2)
                if count % 2:
                    load(first + count - 1, (first + count - 1) % 2, tab[count - 1])

            sp.dma_start(side[:, 0:SMALL], small).then_inc(small_in, 16)
            def load_x(k):
                sp.dma_start(x_sb[:, k * 4 * T:(k + 1) * 4 * T], x_t[:, k * 4 * T:(k + 1) * 4 * T]).then_inc(x_in[k], 16)

            load_x(0)
            load_x(1)
            load(0, 0, w_in[0])
            load_x(2)
            load_x(3)
            load(1, 1, w_in[1])
            sp.dma_start(consts[:, :], id_iota).then_inc(consts_in, 16)
            load_all(w_in[2:N_IN], 2, N_IN - 2)
            sp.wait_ge(conv_ok, CONV_TILES)
            sp.dma_start(key_t, keys).then_inc(keys_in, 16)
            load_all(w_out, C_OUT, KT)
            load_all(w_q, C_WQ, 2 * PEER_HEADS)
            sp.wait_ge(taken, C_WQ)
            sp.dma_start(h_scratch, h_sb).then_inc(h_saved, 16)

            def save_gelu(e, par):
                sp.wait_ge(taken, C_U + 1 + e)
                sp.dma_start(gelu_scratch[e], gelu_out[par]).then_inc(gelu_saved[par], 16)

            LAG = 3
            for e in range(LAG + 1):
                load(C_U + e, (C_U + e) % 2, u_tab[e])
            with sp.Fori(0, (N_KEYS - LAG - 1) // 2) as i:
                for j in range(2):
                    e = 2 * i + j
                    save_gelu(e, (C_U + j) % 2)
                    load(C_U + LAG + 1 + e, (C_U + LAG + 1 + j) % 2, u_tab[LAG + 1 + 2 * i + j])
            def gelu_load(e, par):
                sp.dma_start(gelu_in[par], gelu_scratch[e]).then_inc(gelu_back[par], 16)

            sp.wait_ge(gate_ok, GATE_CHUNKS)
            for j in range(2):
                save_gelu(N_KEYS - LAG - 1 + j, (C_U + LAG + 1 + j) % 2)
                load(C_V_TAB + j, (C_V_TAB + j) % 2, v_tab[j])
                sp.wait_ge(gelu_saved[(C_V_TAB + j) % 2], 16)
                gelu_load(j, (C_V_TAB + j) % 2)
            for e in range(N_KEYS - LAG + 1, N_KEYS):
                save_gelu(e, (C_U + e) % 2)
            for k in range(2):
                sp.wait_ge(gelu_saved[k], 16 * (N_KEYS // 2))
            sp.wait_ge(used, 2 * C_V_TAB)

            def second_table(first, end):
                with sp.Fori(first, end) as i:
                    for j in range(2):
                        par = (C_V_TAB + j) % 2
                        load(C_V_TAB + 2 + 2 * i + j, par, v_tab[2 * i + j + 2])
                        sp.wait_ge(w_ok, 2 * i + j + 1)
                        gelu_load(2 * i + j + 2, par)

            for q in range(H_PARTS + 2):
                second_table(q, q + 1)
                if q < H_PARTS:
                    n = KT * T // H_PARTS
                    sp.dma_start(h_back[:, q * n:(q + 1) * n], h_scratch[:, q * n:(q + 1) * n]).then_inc(h_in, 16)
                else:
                    a, b = (q - H_PARTS) * D // 2, (q - H_PARTS + 1) * D // 2
                    sp.dma_start(g_last[:, a:b], g_f[:, a:b]).then_inc(gf_in, 16)
            second_table(H_PARTS + 2, N_KEYS // 2 - 1)
            for tb in range(TB):
                for q in range(2):
                    sp.wait_ge(last_ok, 2 * tb + q + 1)
                    n = D // 2
                    sp.dma_start(out[tb * P:(tb + 1) * P, q * n:(q + 1) * n],
                                 big[:, (2 * tb + q) * n:(2 * tb + q + 1) * n]).then_inc(stored, 16)
            sp.wait_ge(stored, 16 * 2 * TB)

        @block.gpsimd
        def _(pool):
            pool.wait_ge(squared, 4)
            n, done = KT * T // 2, 0
            while n >= T:
                ins = nc.gpsimd.tensor_tensor(out=sq_sb[:, 0:n], in0=sq_sb[:, 0:n], in1=sq_sb[:, n:2 * n], op=ALU.add)
                ins.then_inc(x_summed, 1)
                n //= 2
                done += 1
                pool.wait_ge(x_summed, done)
            pool.wait_ge(cs_ok, 1)
            pool.wait_ge(consts_in, 16)
            h16 = SSD_HEADS
            nc.gpsimd.tensor_tensor(
                out=cs_rows[0:h16, :].rearrange("p (h m) -> p h m", h=h16),
                in0=cs.rearrange("p (o m) -> p o m", o=1).broadcast_to([h16, h16, BLK]),
                in1=ident[0:h16, 0:h16].rearrange("p (h o) -> p h o", o=1).broadcast_to([h16, h16, BLK]),
                op=ALU.mult).then_inc(rows_ok, 1)

        @block.scalar
        def _(act):
            def cut_high(c, par):
                for half in range(2):
                    s = 2 * par + half
                    act.wait_ge(raw_in[s], 16 * ((c - par) // 2 + 1) if isinstance(c, int) else 8 * (c - par) + 16)
                    if not (isinstance(c, int) and c < 2):
                        act.wait_ge(used, 2 * c + half - 3)
                    nc.scalar.activation(slot(high, s), slot(raw, s), ACT.Copy).then_inc(hi_done, 1)

            def take(c, par, dst, func):
                act.wait_ge(used, 2 * c + 2)
                nc.scalar.activation(dst, ps[:, par, 0:T], func).then_inc(taken, 1)

            def root(k, v, r):
                act.wait_ge(var_ok, k + 1)
                nc.scalar.activation(r, v, ACT.Sqrt).then_inc(root_ok, 1)

            def round_norm(k):
                for q in range(4):
                    act.wait_ge(xn_ok, 4 * k + q + 1)
                    a, b = q * 4 * T, (q + 1) * 4 * T
                    nc.scalar.activation(act_hi[:, a:b], xn_sb[:, a:b], ACT.Copy).then_inc(xh_ok, 1)

            round_norm(0)
            cut_high(0, 0)
            for q in range(4):
                a, b = q * 4 * T, (q + 1) * 4 * T
                nc.scalar.activation(sq_sb[:, a:b], x_sb[:, a:b], ACT.Square).then_inc(squared, 1)
            cut_high(1, 1)
            root(0, rs_v[:, 0:T], rstd1)
            act.wait_ge(small_in, 16)
            act.wait_ge(xl_ok, 4)
            nc.scalar.activation(decay, sm("a_log")[0:SSD_HEADS], ACT.Exp).then_inc(dt_exp, 1)
            act.wait_ge(dt_neg, 1)
            nc.scalar.activation(dtv[2], dtv[1], ACT.Exp).then_inc(dt_exp, 1)
            with act.Fori(0, CONV_TILES // 2) as i:
                for j in range(2):
                    cut_high(C_CONV + 2 * i + j + 1, (C_CONV + j + 1) % 2)
            cut_high(C_K + 1, (C_K + 1) % 2)
            act.wait_ge(conv_ok, CONV_TILES)
            bc = view(XBC + SSD_TILES * T, 2 * GROUPS * T)
            nc.scalar.activation(bc, bc, ACT.Silu).then_inc(silu_ok, 1)
            xs = view(XBC, SSD_TILES * T)
            nc.scalar.activation(xs, xs, ACT.Silu).then_inc(silu_ok, 1)
            cut_high(C_V + 1, (C_V + 1) % 2)
            for b in range(4):
                act.wait_ge(tr_ok, b + 1)
                nc.scalar.activation(x_tok[:, b * 512:(b + 1) * 512], ps[:, 4 + b, :], ACT.Copy).then_inc(tok_ok, 1)

            def ssd_step(s, j):
                c, par = C_Q + s, (C_Q + j) % 2
                for p in range(2):
                    act.wait_ge(seg_ok, 2 * s + p + 1)
                    nc.scalar.activation(expo[p], expo[p], ACT.Exp).then_inc(exp_ok, 1)
                cut_high(c + 1, 1 - par)

            with act.Fori(0, SSD_TILES // 2) as i:
                for j in range(2):
                    ssd_step(2 * i + j, j)

            def scale_q(s, j):
                nc.scalar.activation(q_in[j], big[:, ds(QZ + s * T, T)], ACT.Copy,
                                     scale=float(HEAD_DIM) ** -0.5).then_inc(q_ok, 1)

            def take_pt(s, j):
                act.wait_ge(pt_ok, s + 1)
                nc.scalar.activation(prob_t[j], ps[:, 4:6, 0:BLK], ACT.Copy).then_inc(pt_out, 1)

            def take_o(s):
                act.wait_ge(o_ok, s + 1)
                nc.scalar.activation(big[:, ds(Y_T + SSD_TILES * T + s * T, T)], ps[:, 6, 0:T],
                                     ACT.Copy).then_inc(o_out, 1)

            def att_step(s, j, first=False, last=False):
                cut_high(C_Z + s + 1, (C_Z + j + 1) % 2)
                if not first:
                    take_pt(s - 1, 1 - j)
                act.wait_ge(max_ok, s + 1)
                neg, den, snk = st[j][1], st[j][2], st[j][3]
                for e in range(2):
                    for b, (lo, hi) in enumerate(((0, P), (P, BLK))):
                        n = 2 * b + e
                        nc.scalar.activation(prob[j][:, e, lo:hi], prob[j][:, e, lo:hi], ACT.Exp,
                                             bias=neg[:, n:n + 1], accum_out=den[:, n:n + 1])
                nc.scalar.activation(snk, snk, ACT.Exp).then_inc(p_ok, 1)
                if last:
                    early_z()
                if not first:
                    take_o(s - 1)
                if not last:
                    scale_q(s + 1, 1 - j)

            def square_y(q):
                a, b = q * 4 * T, (q + 1) * 4 * T
                nc.scalar.activation(sq_sb[:, a:b], y_sb[:, a:b], ACT.Square).then_inc(squared, 1)

            z_first = view(QZ + SSD_TILES * T, (SSD_TILES - 1) * T)
            z_last = view(QZ + (2 * SSD_TILES - 1) * T, T)

            def early_z():
                act.wait_ge(taken, C_OUT - 1)
                nc.scalar.activation(z_first, z_first, ACT.Silu).then_inc(z_ok, 1)

            act.wait_ge(y_out, SSD_HEADS)
            act.wait_ge(taken, C_Z)
            scale_q(0, 0)
            att_step(0, 0, True)
            with act.Fori(0, SSD_TILES // 2 - 1) as i:
                for j in range(2):
                    att_step(1 + 2 * i + j, 1 - j)
            att_step(SSD_TILES - 1, 1, last=True)
            act.wait_ge(pn_ok, SSD_TILES)
            take_pt(SSD_TILES - 1, 1)
            act.wait_ge(taken, C_OUT)
            nc.scalar.activation(z_last, z_last, ACT.Silu).then_inc(z_ok, 1)
            take_o(SSD_TILES - 1)
            act.wait_ge(mix_ok, 1)
            square_y(0)
            act.wait_ge(o_out, SSD_TILES)
            square_y(2)
            square_y(3)
            act.wait_ge(mix_ok, 2)
            square_y(1)
            root(1, rs_v[:, 0:T], rs_r[:, 0:T])
            root(2, rs_v[:, T:], rs_r[:, T:])
            round_norm(1)
            def round_tile(m, dst, src):
                nc.scalar.activation(dst[:, ds(m * T, T)], src[:, ds(m * T, T)], ACT.Copy).then_inc(tile_hi, 1)

            def out_step(m, j):
                cut_high(C_OUT + m + 1, (C_OUT + j + 1) % 2)
                act.wait_ge(tile_ok, m + 1)
                round_tile(m, act2_hi, y_sb)
                if not (isinstance(m, int) and m < 2):
                    act.wait_ge(tile_lo, m - 1)
                nc.scalar.activation(h_sq[j], h_sb[:, ds(m * T, T)], ACT.Square).then_inc(h_squared, 1)

            for m in range(2):
                out_step(m, m)
            with act.Fori(1, KT // 2) as i:
                for j in range(2):
                    out_step(2 * i + j, j)
            cut_high(C_WQ + 1, (C_WQ + 1) % 2)
            root(3, rs_v[:, 0:T], rs_r[:, 0:T])

            def query_step(m, j):
                if not (isinstance(m, int) and m > KT - 3):
                    cut_high(C_WQ + m + 2, (C_WQ + j) % 2)
                act.wait_ge(tile_ok, KT + m + 1)
                round_tile(m, act_hi, y_sb)

            with act.Fori(0, KT // 2 - 1) as i:
                for j in range(2):
                    query_step(2 * i + j, j)
            cut_high(C_U, C_U % 2)
            for m in range(KT - 2, KT):
                query_step(m, m % 2)
            act.wait_ge(taken, C_U)

            def expert_step(c, par):
                cut_high(c + 1, 1 - par)
                if not isinstance(c, int) or c >= C_U + 2:
                    act.wait_ge(gelu_saved[par], 8 * (c - C_U - (par - C_U) % 2))
                take(c, par, gelu_out[par], ACT.Gelu)

            for j in range(2):
                expert_step(C_U + j, (C_U + j) % 2)
            with act.Fori(1, ROUTE_CHUNKS // 2) as i:
                for j in range(2):
                    expert_step(C_U + 2 * i + j, (C_U + j) % 2)
            act.wait_ge(soft_in, 1)
            nc.scalar.activation(pick[2], pick[2], ACT.Exp).then_inc(soft_exp, 1)
            act.wait_ge(h_saved, 16)
            with act.Fori(0, GATE_CHUNKS // 2) as i:
                for j in range(2):
                    g = 2 * i + j
                    expert_step(C_U + ROUTE_CHUNKS + g, (C_U + j) % 2)
                    act.wait_ge(gate_ok, g + 1)
                    nc.scalar.activation(
                        big[:, :].rearrange("p (r t) -> p r t", t=T)[:, :, ds(g * TOK_GROUP, TOK_GROUP)],
                        ps[:, 2 + j, :].rearrange("p (t r) -> p r t", r=P), ACT.Copy).then_inc(gate_out, 1)
            first = ROUTE_CHUNKS + GATE_CHUNKS
            with act.Fori(0, (N_KEYS - first) // 2 - 1) as i:
                for j in range(2):
                    expert_step(C_U + first + 2 * i + j, (C_U + j) % 2)

            def round_w(e, par):
                act.wait_ge(w_ok, e + 1)
                if not (isinstance(e, int) and e < 2):
                    act.wait_ge(used, 2 * (C_V_TAB + e - 2) + 2)
                nc.scalar.activation(w_hi[:, par * T:(par + 1) * T], w_full[par], ACT.Copy).then_inc(wh_ok, 1)

            expert_step(C_V_TAB - 2, C_V_TAB % 2)
            expert_step(C_V_TAB - 1, (C_V_TAB + 1) % 2)
            round_w(0, C_V_TAB % 2)
            with act.Fori(0, N_KEYS // 2 - 1) as i:
                for j in range(2):
                    e = 1 + 2 * i + j
                    par = (C_V_TAB + 1 + j) % 2
                    cut_high(C_V_TAB + e, par)
                    round_w(e, par)
            cut_high(C_END - 1, (C_END - 1) % 2)
            round_w(N_KEYS - 1, (C_END - 1) % 2)
            for tb in range(TB):
                act.wait_ge(sum_ok, tb + 1)
                acc = ps[:, 4 * tb:4 * tb + 4, :]
                nc.scalar.activation(big[:, 8192 + tb * D:8192 + (tb + 1) * D].rearrange("p (b n) -> p b n", b=4), acc,
                                     ACT.Square, accum_out=big[:, 16384 + 8 * tb:16385 + 8 * tb]).then_inc(last_sq, 1)
                act.wait_ge(last_var, tb + 1)
                s = 16384 + 8 * tb
                nc.scalar.activation(big[:, s + 2:s + 3], big[:, s + 1:s + 2], ACT.Sqrt).then_inc(last_root, 1)

        @block.vector
        def _(dve):
            own = Order(dve, dve_own)
            V = nc.vector

            def cut_low_piece(c, par, half):
                s = 2 * par + half
                dve.wait_ge(hi_done, 2 * c + half + 1)
                V.tensor_tensor(slot(low, s), slot(raw, s), slot(high, s).bitcast(F32),
                                ALU.subtract).then_inc(lo_done, 1)

            def cut_low(c, par):
                for half in range(2):
                    cut_low_piece(c, par, half)

            def newton(v, r):
                t = v
                own.step(V.reciprocal(r, r))
                own.settle()
                own.step(V.scalar_tensor_tensor(out=t, in0=r, scalar=-0.5, in1=v, op0=ALU.mult, op1=ALU.mult))
                own.settle()
                own.step(V.tensor_tensor(t, t, r, ALU.mult))
                own.settle()
                own.step(V.scalar_tensor_tensor(out=r, in0=t, scalar=1.5, in1=r, op0=ALU.add, op1=ALU.mult))
                own.settle()

            def inverse_root(k, v, r, sums):
                dve.wait_ge(summed, k + 1)
                for bank, n, at, width in sums:
                    ins = V.tensor_scalar(v[:, at:at + n], ps[:, bank, 0:n], 1.0 / width, EPS, ALU.mult, ALU.add)
                ins.then_inc(var_ok, 1)
                dve.wait_ge(root_ok, k + 1)
                newton(v, r)

            def scale_and_cut(k, scale_tile, after_first=None):
                def low_part(q):
                    a, b = q * 4 * T, (q + 1) * 4 * T
                    dve.wait_ge(xh_ok, 4 * k + q + 1)
                    V.tensor_tensor(act_lo[:, a:b], xn_sb[:, a:b], act_hi[:, a:b].bitcast(F32),
                                    ALU.subtract).then_inc(xl_ok, 1)

                for q in range(4):
                    for kk in range(4 * q, 4 * q + 4):
                        ins = scale_tile(kk)
                    ins.then_inc(xn_ok, 1)
                    if q:
                        low_part(q - 1)
                    elif after_first:
                        after_first()
                low_part(3)

            def take(c, par, dst, r, rows=P):
                dve.wait_ge(used, 2 * c + 2)
                V.tensor_tensor(dst, ps[0:rows, par, 0:T], r[0:rows], ALU.mult).then_inc(taken, 1)

            dve.wait_ge(small_in, 16)

            def gain_x(kk):
                if kk % 4 == 0:
                    dve.wait_ge(x_in[kk // 4], 16)
                a, b = kk * T, (kk + 1) * T
                return V.tensor_scalar(xn_sb[:, a:b], x_sb[:, a:b], sm("g1", kk, 1), None, ALU.mult)

            scale_and_cut(0, gain_x)
            cut_low(0, 0)
            V.memset(conv_in[:, :, 0:CONV_W - 1], 0.0).then_inc(pads_ok, 1)
            cut_low(1, 1)
            inverse_root(0, rs_v[:, 0:T], rstd1, [(7, T, 0, D)])
            take(0, 0, dtv[0], rstd1, rows=SSD_HEADS)
            h16 = SSD_HEADS
            dve.wait_ge(taken, 1)
            own.step(V.tensor_scalar(dtv[0], dtv[0], sm("dt_bias")[0:h16], None, ALU.add))
            own.step(V.memset(dtv[5], 1.0))
            own.settle()
            own.step(V.tensor_scalar(dtv[1], dtv[0], -1.0, None, ALU.mult))
            own.settle()
            V.tensor_tensor(dtv[1], dtv[1], dtv[0], ALU.min).then_inc(dt_neg, 1)
            dve.wait_ge(dt_exp, 2)
            own.step(V.tensor_scalar(dtv[3], dtv[2], 2.0, None, ALU.add))
            own.settle()
            own.step(V.reciprocal(dtv[3], dtv[3]))
            own.settle()
            own.step(V.tensor_tensor(dtv[1], dtv[2], dtv[3], ALU.mult))
            own.settle()
            own.step(V.tensor_tensor(dtv[2], dtv[1], dtv[1], ALU.mult))
            own.settle()
            own.step(V.tensor_scalar(dtv[3], dtv[2], 1.0 / 17, None, ALU.mult))
            own.settle()
            for k in range(7, 0, -1):
                own.step(V.scalar_tensor_tensor(out=dtv[3], in0=dtv[3], scalar=1.0 / (2 * k + 1), in1=dtv[2],
                                                op0=ALU.add, op1=ALU.mult))
                own.settle()
            own.step(V.scalar_tensor_tensor(out=dtv[3], in0=dtv[3], scalar=1.0, in1=dtv[1],
                                            op0=ALU.add, op1=ALU.mult))
            own.step(V.tensor_scalar(dtv[0], dtv[0], 0.0, None, ALU.max))
            own.settle()
            dt = dtv[4]
            own.step(V.scalar_tensor_tensor(out=dt, in0=dtv[3], scalar=2.0, in1=dtv[0], op0=ALU.mult, op1=ALU.add))
            own.settle()
            own.step(V.tensor_scalar(dtv[3], dt, decay, -1.0, ALU.mult, ALU.mult))
            own.settle()
            own.step(V.tensor_tensor_scan(cs[:, 0:T], dtv[5], dtv[3], 0.0, ALU.mult, ALU.add))
            V.tensor_tensor_scan(cs[:, T:BLK], dtv[5][:, 0:P], dtv[3][:, P:T], 0.0, ALU.mult,
                                 ALU.add).then_inc(cs_ok, 1)

            with dve.Fori(0, CONV_TILES // 2) as i:
                own.enter(i, 3 * 2)
                for j in range(2):
                    m = 2 * i + j
                    c, par = C_CONV + 2 * i + j, (C_CONV + j) % 2
                    cut_low(c + 1, 1 - par)
                    take(c, par, big[:, ds(CONV_IN + CONV_W - 1 + m * UP, T)], rstd1)
                    dve.wait_ge(taken, c + 1)
                    wc, bc = _small["conv_w"][0], _small["conv_b"][0]
                    dst = big[:, ds(XBC + m * T, T)]
                    for w in range(CONV_W):
                        src = big[:, ds(CONV_IN + w + m * UP, T)]
                        tap = side[:, ds(wc + w + m * CONV_W, 1)]
                        if w == 0:
                            ins = V.tensor_scalar(dst, src, tap, side[:, ds(bc + m, 1)], ALU.mult, ALU.add)
                        else:
                            ins = V.scalar_tensor_tensor(out=dst, in0=src, scalar=tap, in1=dst,
                                                         op0=ALU.mult, op1=ALU.add)
                        if w < CONV_W - 1:
                            own.step(ins)
                            own.settle()
                    ins.then_inc(conv_ok, 1)
            own.leave(CONV_TILES // 2)
            cut_low(C_K + 1, (C_K + 1) % 2)
            take(C_K, C_K % 2, k_t, rstd1)
            cut_low(C_V + 1, (C_V + 1) % 2)
            take(C_V, C_V % 2, v_t, rstd1)
            for g in range(GROUPS):
                dve.wait_ge(cb_ok, g + 1)
                V.tensor_tensor(cb_m[g], ps[:, 2 + g, 0:BLK], sm("tri"), ALU.mult).then_inc(cbm_ok, 1)
            dve.wait_ge(small_t, 1)
            V.tensor_copy(tok_t, ps[:, 2, 0:4 * h16])
            V.tensor_copy(v_tok, ps[:, 3, 0:TB * P]).then_inc(small_t, 1)
            dve.wait_ge(small_t, 2)
            dve.wait_ge(cbm_ok, GROUPS)
            dve.wait_ge(tok_ok, 4)

            def seg(h, p):
                dve.wait_ge(bc_ok, h + 1)
                for b, (lo, hi) in enumerate(((0, T), (T, BLK))):
                    ins = V.tensor_scalar(expo[p][:, lo:hi], ps[:, 2 + p, lo:hi],
                                          big[:, ds(TAIL + 2 * BLK + 3 * T + b * h16 + h, 1)], 0.0,
                                          ALU.subtract, ALU.min)
                ins.then_inc(seg_ok, 1)

            def weigh(h, p, s):
                dve.wait_ge(exp_ok, h + 1)
                if not (isinstance(h, int) and h < 2):
                    dve.wait_ge(y_ok, h - 1)
                steps = SSD_TILES // GROUPS
                V.tensor_tensor(m_sb[p], expo[p], big[:, ds(TAIL + (s // steps) * BLK, BLK)], ALU.mult)
                for b in range(TB):
                    ins = V.tensor_scalar(xdt[p][:, b * HEAD_DIM:(b + 1) * HEAD_DIM],
                                          big[:, ds(X_TOK + b * D_SSD + h * HEAD_DIM, HEAD_DIM)],
                                          big[:, ds(TAIL + 2 * BLK + 3 * T + (2 + b) * h16 + h, 1)], None, ALU.mult)
                ins.then_inc(m_ok, 1)

            def y_take(h, pair, p):
                dve.wait_ge(y_ok, h + 1)
                r0 = p * HEAD_DIM
                rows = slice(r0, r0 + HEAD_DIM)
                V.scalar_tensor_tensor(out=big[rows, ds(Y_T + pair * T, T)], in0=big[rows, ds(XBC + pair * T, T)],
                                       scalar=side[rows, ds(_small["d_skip"][0] + pair, 1)],
                                       in1=ps[rows, 4 + p, 0:T], op0=ALU.mult, op1=ALU.add).then_inc(y_out, 1)

            def ssd_step(s, j, first=False):
                c = C_Q + s + 1
                for p in range(2):
                    seg(2 * s + p, p)
                cut_low_piece(c, (C_Q + j + 1) % 2, 0)
                weigh(2 * s, 0, s)
                weigh(2 * s + 1, 1, s)
                cut_low_piece(c, (C_Q + j + 1) % 2, 1)
                if not first:
                    for p in range(2):
                        y_take(2 * s - 2 + p, s - 1, p)
                take(c - 1, (C_Q + j) % 2, big[:, ds(QZ + s * T, T)], rstd1)

            for s in range(2):
                ssd_step(s, s, s == 0)
            with dve.Fori(1, SSD_TILES // 2) as i:
                for j in range(2):
                    ssd_step(2 * i + j, j)
            for p in range(2):
                y_take(SSD_HEADS - 2 + p, SSD_TILES - 1, p)

            def att_step(s, j, last=False):
                c = C_Z + s + 1
                mx, neg, den, snk, rec = st[j]
                dve.wait_ge(logit_ok, s + 1)
                win = sm("window").rearrange("p (o m) -> p o m", o=1).broadcast_to([P, 2, BLK])
                own.step(V.tensor_tensor(prob[j], ps[:, 2:4, 0:BLK], win, ALU.add))
                own.settle()
                own.step(V.tensor_reduce(mx[:, 0:2], prob[j][:, :, 0:P], AX, ALU.max))
                own.step(V.tensor_reduce(mx[:, 2:4], prob[j][:, :, P:BLK], AX, ALU.max))
                own.settle()
                sink = side[:, ds(_small["sinks"][0] + s * 2, 2)]
                sink2 = sink.rearrange("p (o e) -> p o e", o=1).broadcast_to([P, 2, 2])
                four = lambda t: t.rearrange("p (b e) -> p b e", e=2)
                own.step(V.tensor_tensor(four(mx), four(mx), sink2, ALU.max))
                own.settle()
                own.step(V.tensor_scalar(neg, mx, -1.0, None, ALU.mult))
                own.settle()
                V.tensor_tensor(four(snk), four(neg), sink2, ALU.add).then_inc(max_ok, 1)
                cut_low(c, (C_Z + j + 1) % 2)
                dve.wait_ge(p_ok, s + 1)
                own.step(V.tensor_tensor(den, den, snk, ALU.add))
                own.settle()
                own.step(V.reciprocal(rec, den))
                own.settle()
                for b, (lo, hi) in enumerate(((0, P), (P, BLK))):
                    part = prob[j][:, :, lo:hi]
                    ins = V.tensor_tensor(part, part, rec[:, 2 * b:2 * b + 2].rearrange(
                        "p (e o) -> p e o", o=1).broadcast_to([P, 2, hi - lo]), ALU.mult)
                    if b == 0:
                        own.step(ins)
                ins.then_inc(pn_ok, 1)
                if last:
                    gate_y(0, SSD_TILES - 1)
                take(c - 1, (C_Z + j) % 2, big[:, ds(QZ + (SSD_TILES + s) * T, T)], rstd1)

            def gate_y(lo, hi):
                dve.wait_ge(z_ok, 1 if lo == 0 else 2)
                dve.wait_ge(y_out, SSD_HEADS)
                y = y_sb[:, lo * T:hi * T]
                V.tensor_tensor(y, y, view(QZ + (SSD_TILES + lo) * T, (hi - lo) * T), ALU.mult).then_inc(mix_ok, 1)

            with dve.Fori(0, SSD_TILES // 2 - 1) as i:
                own.enter(i, 2 * 8)
                for j in range(2):
                    att_step(2 * i + j, j)
            own.leave(SSD_TILES // 2 - 1)
            att_step(SSD_TILES - 2, 0)
            att_step(SSD_TILES - 1, 1, last=True)
            gate_y(SSD_TILES - 1, SSD_TILES)
            half = SSD_TILES // GROUPS
            def scale_y(kk):
                a, b, n = kk * T, (kk + 1) * T, min(kk // half, 2)
                return V.scalar_tensor_tensor(out=xn_sb[:, a:b], in0=y_sb[:, a:b], scalar=sm("g_mix", kk, 1),
                                              in1=rs_r[:, n * T:(n + 1) * T], op0=ALU.mult, op1=ALU.mult)

            inverse_root(1, rs_v[:, 0:T], rs_r[:, 0:T], [(7, T, 0, D_SSD // GROUPS)])
            scale_and_cut(1, scale_y, lambda: inverse_root(
                2, rs_v[:, T:], rs_r[:, T:], [(3, T, 0, D_SSD // GROUPS), (2, T, T, D - D_SSD)]))

            def tile_low(m, k, hi, lo):
                dve.wait_ge(tile_hi, k + 1)
                V.tensor_tensor(lo[:, ds(m * T, T)], y_sb[:, ds(m * T, T)], hi[:, ds(m * T, T)].bitcast(F32),
                                ALU.subtract).then_inc(tile_lo, 1)

            def add_square(m, p):
                dve.wait_ge(h_squared, m + 1)
                own.settle()
                own.step(V.tensor_tensor(h_sum, h_sum, h_sq[p], ALU.add))

            def out_step(m, j, first=False):
                c, par = C_OUT + m, (C_OUT + j) % 2
                cut_low(c + 1, 1 - par)
                if not first:
                    add_square(m - 1, 1 - j)
                    tile_low(m - 1, m - 1, act2_hi, act2_lo)
                dve.wait_ge(used, 2 * c + 2)
                V.tensor_tensor(h_sb[:, ds(m * T, T)], ps[:, par, 0:T], x_sb[:, ds(m * T, T)], ALU.add).then_inc(taken, 1)
                dve.wait_ge(taken, c + 1)
                V.tensor_scalar(y_sb[:, ds(m * T, T)], h_sb[:, ds(m * T, T)],
                                side[:, ds(_small["g2"][0] + m, 1)], None, ALU.mult).then_inc(tile_ok, 1)

            own.step(V.memset(h_sum, 0.0))
            out_step(0, 0, True)
            out_step(1, 1)
            with dve.Fori(1, KT // 2) as i:
                own.enter(i - 1, 2)
                for j in range(2):
                    out_step(2 * i + j, j)
            own.leave(KT // 2 - 1)
            dve.wait_ge(h_squared, KT)
            own.settle()
            V.tensor_tensor(h_sum, h_sum, h_sq[1], ALU.add).then_inc(h_summed, 1)
            tile_low(KT - 1, KT - 1, act2_hi, act2_lo)
            cut_low(C_WQ + 1, (C_WQ + 1) % 2)
            inverse_root(3, rs_v[:, 0:T], rs_r[:, 0:T], [(7, T, 0, D)])

            def score_take(m, j):
                dve.wait_ge(score_ok, m + 1)
                dst = view(SCORES, TB * 2 * PEER_HEADS * N_KEYS).rearrange("p (b m) -> p b m", b=TB)
                V.tensor_copy(dst[:, :, ds(m * N_KEYS, N_KEYS)],
                              ps[:, 2 + j, 0:TB * N_KEYS].rearrange("p (b n) -> p b n", b=TB)).then_inc(score_out, 1)

            def query_step(m, j):
                start = isinstance(m, int)
                if not (start and m < 2):
                    dve.wait_ge(score_ok, m - 1)
                take(C_WQ + m, (C_WQ + j) % 2, q_t[j], rs_r[:, 0:T])
                if not (start and m > KT - 2):
                    cut_low(C_WQ + m + 2, (C_WQ + j) % 2)
                if not (start and m == 0):
                    score_take(m - 1, 1 - j)
                y = y_sb[:, ds(m * T, T)]
                V.tensor_tensor(y, y, rs_r[:, 0:T], ALU.mult).then_inc(tile_ok, 1)
                if not (start and m == 0):
                    tile_low(m - 1, KT + m - 1, act_hi, act_lo)

            for m in range(2):
                query_step(m, m)
            with dve.Fori(1, KT // 2 - 1) as i:
                for j in range(2):
                    query_step(2 * i + j, j)
            for m in range(KT - 2, KT):
                query_step(m, m % 2)
            score_take(KT - 1, 1)
            tile_low(KT - 1, 2 * KT - 1, act_hi, act_lo)
            dve.wait_ge(score_out, 2 * PEER_HEADS)
            dve.wait_ge(consts_in, 16)
            iota16 = iota[:, 0:TOPK].rearrange("p (o a) -> p o a", o=1).broadcast_to([P, TOPK, TOPK])

            def best(src, spare, vals, idx, k):
                if k == 0:
                    own.step(V.max(vals[:, 0:8], src))
                elif k == 1:
                    own.step(V.max_index(idx[:, 0:8], vals[:, 0:8], src))
                    own.step(V.match_replace(spare, vals[:, 0:8], src, LOWEST))
                elif k == 2:
                    own.step(V.max(vals[:, 8:16], spare))
                else:
                    own.step(V.max_index(idx[:, 8:16], vals[:, 8:16], spare))

            def met():
                V.memset(r_mark, 0.0)

            PER = 27
            def route(i, rr):
                r = 2 * i + rr

                def cut(n):
                    k = ROUTE_SPAN * rr + 1 + n // 2
                    cut_low_piece(C_U + 2 * ROUTE_SPAN * i + k, (C_U + k) % 2, n % 2)

                own.step(V.tensor_copy(r_s.rearrange("p s n -> p (s n)"), big[:, ds(SCORES + r * 2 * N_KEYS, 2 * N_KEYS)]))
                own.settle()
                for k in range(4):
                    met()
                    for s in range(2):
                        best(r_s[:, s], r_s2[:, s], r_v[:, s * TOPK:(s + 1) * TOPK], r_ix[:, s * TOPK:(s + 1) * TOPK], k)
                    if k == 1:
                        cut(0)
                    own.settle()
                cut(1)
                own.step(V.tensor_copy(r_ixf, r_ix))
                va = r_v[:, 0:TOPK].rearrange("p (a o) -> p a o", o=1).broadcast_to([P, TOPK, TOPK])
                vb = r_v[:, TOPK:2 * TOPK].rearrange("p (o b) -> p o b", o=1).broadcast_to([P, TOPK, TOPK])
                own.step(V.tensor_tensor(r_c.rearrange("p (a b) -> p a b", a=TOPK), va, vb, ALU.add))
                own.settle()
                for k in range(4):
                    met()
                    best(r_c, r_c2, r_tv, r_tp, k)
                    if k == 1:
                        cut(2)
                    own.settle()
                cut(3)
                own.step(V.tensor_scalar(r_ab[0], r_tp, 4, None, ALU.logical_shift_right))
                own.step(V.tensor_scalar(r_ab[1], r_tp, TOPK - 1, None, ALU.bitwise_and))
                own.step(V.tensor_copy(big[:, ds(PICKS + 512 + r * TOPK, TOPK)], r_tv))
                own.settle()
                for s in range(2):
                    own.step(V.tensor_tensor(r_eq[s], iota16, r_ab[s].rearrange("p (k o) -> p k o", o=1).broadcast_to(
                        [P, TOPK, TOPK]), ALU.is_equal))
                own.settle()
                for s in range(2):
                    own.step(V.tensor_tensor(r_eq[s], r_eq[s], r_ixf[:, s * TOPK:(s + 1) * TOPK].rearrange(
                        "p (o a) -> p o a", o=1).broadcast_to([P, TOPK, TOPK]), ALU.mult))
                cut(4)
                own.settle()
                for s in range(2):
                    own.step(V.tensor_reduce(big[:, ds(PICKS + s * 256 + r * TOPK, TOPK)], r_eq[s], AX, ALU.add))
                cut(5)
                own.settle()

            with dve.Fori(0, ROUTE_STEPS // 2) as i:
                own.enter(i, 2 * PER)
                for rr in range(2):
                    route(i, rr)
            own.leave(ROUTE_STEPS // 2)
            by_pick = lambda t: t.rearrange("p (s k) -> p s k", k=TOPK)
            gates = by_pick(pick[2])
            wide = lambda t: t.broadcast_to([P, ROUTE_STEPS, TOPK])
            own.step(V.tensor_copy(r_sum, gates[:, :, 0:1].rearrange("p s k -> p (s k)")))
            own.settle()
            V.tensor_tensor(gates, gates, wide(r_sum.rearrange("p (s o) -> p s o", o=1)), ALU.subtract).then_inc(soft_in, 1)
            dve.wait_ge(soft_exp, 1)
            own.step(V.tensor_reduce(r_sum, gates, AX, ALU.add))
            own.settle()
            own.step(V.reciprocal(r_sum, r_sum))
            own.settle()
            V.tensor_tensor(gates, gates, wide(r_sum.rearrange("p (s o) -> p s o", o=1)), ALU.mult).then_inc(picks_ok, 1)
            dve.wait_ge(picks_tr, 1)
            for tb in range(TB):
                own.step(V.tensor_copy(pick_t[:, :].rearrange("p (a t) -> p a t", a=3)[:, :, tb * P:(tb + 1) * P],
                                       ps[:, 4 + tb, 0:3 * P].rearrange("p (a t) -> p a t", a=3)))
            own.settle()
            def spread_round(i, first=False):
                for j in range(2):
                    g = 2 * i + j
                    if not (first and j == 0):
                        dve.wait_ge(gate_ok, g)
                    for t in range(TOK_GROUP):
                        at = g * TOK_GROUP + t
                        V.tensor_scalar(hot_col[:, t * P:(t + 1) * P], iota, pick_t[:, ds(at + T, 1)], None, ALU.is_equal)
                        ins = V.tensor_scalar(hot_row[:, t * P:(t + 1) * P], iota, pick_t[:, ds(at, 1)],
                                              pick_t[:, ds(at + 2 * T, 1)], ALU.is_equal, ALU.mult)
                    ins.then_inc(hot_ok, 1)
                    cut_low(C_U + ROUTE_CHUNKS + g + 1, (C_U + j + 1) % 2)

            spread_round(0, True)
            with dve.Fori(1, GATE_CHUNKS // 2) as i:
                spread_round(i)
            first = ROUTE_CHUNKS + GATE_CHUNKS
            with dve.Fori(0, (N_KEYS - first) // 2 - 1) as i:
                for j in range(2):
                    cut_low(C_U + first + 2 * i + j + 1, (C_U + j + 1) % 2)

            def weights(e, par, between):
                dve.wait_ge(gelu_back[par], 8 * (e + 2 - (par - C_V_TAB) % 2))
                own_gate = big[:, ds(e * T, T)]
                V.tensor_tensor(w_full[par], own_gate, gelu_in[par], ALU.mult).then_inc(w_ok, 1)
                between()
                dve.wait_ge(wh_ok, e + 1)
                V.tensor_tensor(w_lo[:, par * T:(par + 1) * T], w_full[par], w_hi[:, par * T:(par + 1) * T].bitcast(F32),
                                ALU.subtract).then_inc(wl_ok, 1)

            cut_low(C_V_TAB - 1, (C_V_TAB + 1) % 2)
            cut_low(C_V_TAB, C_V_TAB % 2)
            dve.wait_ge(gate_out, GATE_CHUNKS)
            weights(0, C_V_TAB % 2, lambda: None)

            def v_step(e, par):
                cut_low_piece(C_V_TAB + e, par, 0)
                weights(e, par, lambda: cut_low_piece(C_V_TAB + e, par, 1))

            with dve.Fori(0, N_KEYS // 2 - 1) as i:
                for j in range(2):
                    v_step(1 + 2 * i + j, (C_V_TAB + 1 + j) % 2)
            v_step(N_KEYS - 1, (C_END - 1) % 2)
            dve.wait_ge(gf_in, 16 * 2)
            for tb in range(TB):
                s = 16384 + 8 * tb
                dve.wait_ge(last_sq, tb + 1)
                V.tensor_scalar(big[:, s + 1:s + 2], big[:, s:s + 1], 1.0 / D, EPS, ALU.mult, ALU.add).then_inc(last_var, 1)
                dve.wait_ge(last_root, tb + 1)
                newton(big[:, s + 1:s + 2], big[:, s + 2:s + 3])
                for q in range(2):
                    n = D // 2
                    V.scalar_tensor_tensor(
                        out=big[:, (2 * tb + q) * n:(2 * tb + q + 1) * n].rearrange("p (b n) -> p b n", b=2),
                        in0=ps[:, 4 * tb + 2 * q:4 * tb + 2 * q + 2, :], scalar=big[:, s + 2:s + 3],
                        in1=g_last[:, q * n:(q + 1) * n].rearrange("p (b n) -> p b n", b=2),
                        op0=ALU.mult, op1=ALU.mult).then_inc(last_ok, 1)

        @block.tensor
        def _(pe):
            mm = nc.tensor.matmul

            def product(c, par, midway=None, ins_hi=None, ins_lo=None, ready=None):
                if not (isinstance(c, int) and c < 2):
                    pe.wait_ge(taken, c - 1)
                acc = ps[:, par, 0:T]
                src_hi, src_lo = (act_hi, act_lo) if ins_hi is None else (ins_hi, ins_lo)
                for half in range(2):
                    s = 2 * par + half
                    pe.wait_ge(lo_done, 2 * c + half + 1)
                    if ready:
                        pe.wait_ge(ready[0], ready[1 + half])
                    for k in range(8):
                        kk = 8 * half + k
                        a_hi, a_lo = src_hi[:, kk * T:(kk + 1) * T], src_lo[:, kk * T:(kk + 1) * T]
                        wh = high[:, s * PIECE + k * P:s * PIECE + (k + 1) * P]
                        wl = low[:, s * PIECE + k * P:s * PIECE + (k + 1) * P]
                        mm(acc, wh, a_hi, start=(kk == 0), stop=False)
                        mm(acc, wh, a_lo, start=False, stop=False)
                        ins = mm(acc, wl, a_hi, start=False, stop=(kk == KT - 1))
                    ins.then_inc(used, 1)
                    if midway and half == 0:
                        midway()

            def sum_tiles(bank, lo, tiles, src, start=True, stop=True):
                for n, t in enumerate(tiles):
                    ins = mm(ps[:, bank, lo:lo + T], sm("ones"), src[:, t * T:(t + 1) * T],
                             start=start and n == 0, stop=stop and n == len(tiles) - 1, skip_group_check=True)
                return ins

            product(0, 0, ready=(xl_ok, 2, 4))
            pe.wait_ge(small_in, 16)
            pe.wait_ge(x_summed, 4)
            sum_tiles(7, 0, [0], sq_sb).then_inc(summed, 1)
            for c in range(1, 3):
                product(c, c % 2)
            with pe.Fori(0, (C_Q - 3) // 2) as i:
                for j in range(2):
                    product(3 + 2 * i + j, (3 + j) % 2)
            pe.wait_ge(silu_ok, 1)
            tile = lambda n: view(XBC + n * T, T)
            for g in range(GROUPS):
                b_t, c_t = tile(SSD_TILES + g), tile(SSD_TILES + GROUPS + g)
                mm(ps[:, 2 + g, 0:T], b_t[:, 0:P], c_t, start=True, stop=True)
                mm(ps[:, 2 + g, T:BLK], b_t[:, P:T], c_t[:, P:T], start=True, stop=True).then_inc(cb_ok, 1)
            pe.wait_ge(silu_ok, 2)
            pe.wait_ge(consts_in, 16)
            for b in range(4):
                for n in range(4):
                    tb, ch = (4 * b + n) // SSD_TILES, (4 * b + n) % SSD_TILES
                    ins = nc.tensor.transpose(ps[:, 4 + b, n * P:(n + 1) * P], tile(ch)[:, tb * P:(tb + 1) * P], ident)
                ins.then_inc(tr_ok, 1)
            pe.wait_ge(cs_ok, 1)
            pe.wait_ge(cbm_ok, GROUPS)
            h16 = SSD_HEADS
            for n, rows in enumerate((cs[:, 0:P], cs[:, T:BLK], dtv[4][:, 0:P], dtv[4][:, P:T])):
                nc.tensor.transpose(ps[:, 2, n * h16:(n + 1) * h16], rows, ident[0:h16, 0:h16])
            pe.wait_ge(taken, C_V + 1)
            for tb in range(TB):
                ins = nc.tensor.transpose(ps[:, 3, tb * P:(tb + 1) * P], v_t[:, tb * P:(tb + 1) * P], ident)
            ins.then_inc(small_t, 1)
            pe.wait_ge(rows_ok, 1)
            pe.wait_ge(small_t, 2)
            pe.wait_ge(tok_ok, 4)

            def spread(h, p):
                if not (isinstance(h, int) and h < 2):
                    pe.wait_ge(seg_ok, h - 1)
                mm(ps[:, 2 + p, 0:BLK], sm("ones")[0:h16, :], cs_rows_at(h), start=True, stop=True).then_inc(bc_ok, 1)

            def cs_rows_at(h):
                return big[0:h16, ds(SQ + h * BLK, BLK)]

            def y_of(h, p):
                pe.wait_ge(m_ok, h + 1)
                if not (isinstance(h, int) and h < 2):
                    pe.wait_ge(y_out, h - 1)
                dst = ps[p * HEAD_DIM:(p + 1) * HEAD_DIM, 4 + p, 0:T]
                mm(dst, xdt[p][:, 0:HEAD_DIM], m_sb[p][:, 0:T], start=True, stop=True)
                mm(dst[:, P:T], xdt[p][:, HEAD_DIM:P], m_sb[p][:, T:BLK], start=False, stop=True,
                   skip_group_check=True).then_inc(y_ok, 1)

            def ssd_step(s, j, first=False):
                if not first:
                    for p in range(2):
                        y_of(2 * s - 2 + p, p)
                for p in range(2):
                    spread(2 * s + p, p)
                product(C_Q + s, (C_Q + j) % 2)

            for s in range(2):
                ssd_step(s, s, s == 0)
            with pe.Fori(1, SSD_TILES // 2) as i:
                for j in range(2):
                    ssd_step(2 * i + j, j)
            for p in range(2):
                y_of(SSD_HEADS - 2 + p, p)
            pe.wait_ge(y_out, SSD_HEADS)

            def logits(s, j):
                pe.wait_ge(q_ok, s + 1)
                for e in range(2):
                    rows = slice(e * HEAD_DIM, (e + 1) * HEAD_DIM)
                    q, kk = q_in[j][rows], k_t[rows]
                    mm(ps[:, 2 + e, 0:P], q[:, 0:P], kk[:, 0:P], start=True, stop=True)
                    ins = mm(ps[:, 2 + e, P:BLK], q[:, P:T], kk, start=True, stop=True)
                ins.then_inc(logit_ok, 1)

            def turn(s, j):
                pe.wait_ge(pn_ok, s + 1)
                for e in range(2):
                    for m in range(3):
                        ins = nc.tensor.transpose(ps[:, 4 + e, m * P:(m + 1) * P],
                                                  prob[j][:, e, m * P:(m + 1) * P], ident)
                ins.then_inc(pt_ok, 1)

            def mix_v(s, j):
                pe.wait_ge(pt_out, s + 1)
                for e in range(2):
                    dst = ps[e * HEAD_DIM:(e + 1) * HEAD_DIM, 6, :]
                    v = [v_tok[:, b * P + e * HEAD_DIM:b * P + (e + 1) * HEAD_DIM] for b in range(TB)]
                    pt = prob_t[j][:, e]
                    mm(dst[:, 0:P], v[0], pt[:, 0:P], start=True, stop=True)
                    mm(dst[:, P:T], v[0], pt[:, P:T], start=True, stop=False)
                    ins = mm(dst[:, P:T], v[1], pt[:, T:BLK], start=False, stop=True)
                ins.then_inc(o_ok, 1)

            def att_step(s, j, first=False):
                if first:
                    logits(s, j)
                    product(C_Z + s, (C_Z + j) % 2)
                else:
                    turn(s - 1, 1 - j)
                    logits(s, j)
                    product(C_Z + s, (C_Z + j) % 2, lambda: (late_o(s), mix_v(s - 1, 1 - j)))

            def late_o(s):
                if not (isinstance(s, int) and s < 2):
                    pe.wait_ge(o_out, s - 1)

            att_step(0, 0, True)
            att_step(1, 1)
            with pe.Fori(1, SSD_TILES // 2) as i:
                for j in range(2):
                    att_step(2 * i + j, j)
            turn(SSD_TILES - 1, 1)
            late_o(SSD_TILES)
            mix_v(SSD_TILES - 1, 1)
            half = SSD_TILES // GROUPS
            pe.wait_ge(squared, 5)
            sum_tiles(7, 0, range(half), sq_sb).then_inc(summed, 1)
            pe.wait_ge(squared, 6)
            sum_tiles(2, 0, range(2 * half, 3 * half), sq_sb, stop=False)
            pe.wait_ge(squared, 7)
            sum_tiles(2, 0, range(3 * half, KT), sq_sb, start=False)
            pe.wait_ge(squared, 8)
            sum_tiles(3, 0, range(half, 2 * half), sq_sb).then_inc(summed, 1)
            product(C_OUT, C_OUT % 2, ready=(xl_ok, 6, 8))
            product(C_OUT + 1, (C_OUT + 1) % 2)
            with pe.Fori(1, KT // 2) as i:
                for j in range(2):
                    product(C_OUT + 2 * i + j, (C_OUT + j) % 2)
            query = dict(ins_hi=act2_hi, ins_lo=act2_lo)
            product(C_WQ, C_WQ % 2, ready=(tile_lo, KT // 2, KT), **query)
            pe.wait_ge(h_summed, 1)
            sum_tiles(7, 0, [0], h_sum).then_inc(summed, 1)
            pe.wait_ge(keys_in, 16)

            def scores(m, j):
                pe.wait_ge(taken, C_WQ + 1 + m)
                if not (isinstance(m, int) and m < 2):
                    pe.wait_ge(score_out, m - 1)
                for tb in range(TB):
                    ins = mm(ps[:, 2 + j, tb * N_KEYS:(tb + 1) * N_KEYS], q_t[j][:, tb * P:(tb + 1) * P],
                             big[:, ds(CONV_IN + m * N_KEYS, N_KEYS)], start=True, stop=True)
                ins.then_inc(score_ok, 1)

            for j in range(2):
                product(C_WQ + 1 + j, (C_WQ + 1 + j) % 2, **query)
                scores(j, j)
            with pe.Fori(1, PEER_HEADS - 1) as i:
                for j in range(2):
                    product(C_WQ + 1 + 2 * i + j, (C_WQ + 1 + j) % 2, **query)
                    scores(2 * i + j, j)
            product(C_U - 1, (C_U - 1) % 2, **query)
            scores(2 * PEER_HEADS - 2, 0)
            scores(2 * PEER_HEADS - 1, 1)
            product(C_U, C_U % 2, ready=(tile_lo, KT + KT // 2, 2 * KT))
            product(C_U + 1, (C_U + 1) % 2)
            with pe.Fori(1, ROUTE_CHUNKS // 2) as i:
                for j in range(2):
                    product(C_U + 2 * i + j, (C_U + j) % 2)
            pe.wait_ge(picks_ok, 1)
            for tb in range(TB):
                for a in range(3):
                    ins = nc.tensor.transpose(ps[:, 4 + tb, a * P:(a + 1) * P], pick[a][:, tb * P:(tb + 1) * P], ident)
            ins.then_inc(picks_tr, 1)
            def gate_round(i, first=False):
                for j in range(2):
                    g = 2 * i + j
                    product(C_U + ROUTE_CHUNKS + g, (C_U + j) % 2)
                    pe.wait_ge(hot_ok, g + 1)
                    if not first:
                        pe.wait_ge(gate_out, g - 1)
                    for t in range(TOK_GROUP):
                        ins = mm(ps[:, 2 + j, t * P:(t + 1) * P], hot_col[:, t * P:(t + 1) * P],
                                 hot_row[:, t * P:(t + 1) * P], start=True, stop=True)
                    ins.then_inc(gate_ok, 1)

            gate_round(0, True)
            with pe.Fori(1, GATE_CHUNKS // 2) as i:
                gate_round(i)
            first = ROUTE_CHUNKS + GATE_CHUNKS
            with pe.Fori(0, (N_KEYS - first) // 2) as i:
                for j in range(2):
                    product(C_U + first + 2 * i + j, (C_U + j) % 2)
            pe.wait_ge(taken, C_V_TAB)
            pe.wait_ge(gate_out, GATE_CHUNKS)

            def row_products(par, hf, tb, start=False, stop=False):
                s = 2 * par + hf
                at = par * T + tb * P
                wh, wl = w_hi[:, at:at + P], w_lo[:, at:at + P]
                vh = [high[:, s * PIECE + n * 512:s * PIECE + (n + 1) * 512] for n in range(2)]
                vl = [low[:, s * PIECE + n * 512:s * PIECE + (n + 1) * 512] for n in range(2)]
                acc = [ps[:, 4 * tb + 2 * hf + n, :] for n in range(2)]
                for n in range(2):
                    mm(acc[n], wh, vh[n], start=start, stop=False, skip_group_check=True)
                for n in range(2):
                    mm(acc[n], wh, vl[n], start=False, stop=False, skip_group_check=True)
                for n in range(2):
                    ins = mm(acc[n], wl, vh[n], start=False, stop=stop, skip_group_check=True)
                return ins

            def expert_rows(e, par, start=False):
                c = C_V_TAB + e
                pe.wait_ge(wl_ok, e + 1)
                for hf in range(2):
                    pe.wait_ge(lo_done, 2 * c + hf + 1)
                    for tb in range(TB):
                        ins = row_products(par, hf, tb, start=start)
                    ins.then_inc(used, 1)

            for j in range(2):
                expert_rows(j, (C_V_TAB + j) % 2, start=(j == 0))
            with pe.Fori(1, N_KEYS // 2 - 1) as i:
                for j in range(2):
                    expert_rows(2 * i + j, (C_V_TAB + j) % 2)
            expert_rows(N_KEYS - 2, (C_END - 2) % 2)
            pe.wait_ge(h_in, 16 * H_PARTS)
            e, par = N_KEYS - 1, (C_END - 1) % 2
            pe.wait_ge(wl_ok, N_KEYS)
            pe.wait_ge(lo_done, 2 * C_END)
            for tb in range(TB):
                for k in range(KT):
                    mm(ps[:, 4 * tb + k // 4, (k % 4) * P:(k % 4 + 1) * P],
                       h_back[:, k * T + tb * P:k * T + (tb + 1) * P], ident, start=False, stop=False,
                       skip_group_check=True)
                for hf in range(2):
                    ins = row_products(par, hf, tb, stop=True)
                ins.then_inc(sum_ok, 1)


def kernel(x, norm1_g, w_in, conv_w, conv_b, dt_bias, a_log, d_skip, ssd_norm_g, attn_sinks, attn_norm_g,
           w_out, norm2_g, peer_wq, peer_keys, peer_u, peer_v, norm_f_g):
    import numpy as np
    import concourse.bacc as bacc
    from concourse.bass_utils import run_bass_kernel_spmd

    f32 = np.float32
    arr = lambda a: np.asarray(a)
    conv_dim = CONV_TILES * P
    kv = 2 * HEAD_DIM
    o_z, o_xbc = 0, D_SSD
    o_dt = o_xbc + conv_dim
    o_q = o_dt + SSD_HEADS
    o_k = o_q + D - D_SSD
    o_v = o_k + kv
    heads = np.arange(SSD_HEADS).reshape(2, SSD_TILES).T.ravel()
    att = (heads[:, None] * HEAD_DIM + np.arange(HEAD_DIM)).ravel()

    def chunks(w):
        return np.ascontiguousarray(w.reshape(KT, P, -1, P).transpose(2, 1, 0, 3)).reshape(-1, P, D)

    wi = arr(w_in)[0]
    dt_cols = np.zeros((D, P), f32)
    dt_cols[:, :SSD_HEADS] = wi[:, o_dt:o_q]
    wi = np.concatenate([dt_cols, wi[:, o_xbc:o_dt], wi[:, o_k:o_v], wi[:, o_v:o_v + kv], wi[:, o_q + att],
                         wi[:, o_z:o_xbc]], axis=1)
    wo = arr(w_out)[0]
    wo = np.concatenate([wo[:D_SSD], wo[D_SSD + att]], axis=0)
    cols = lambda a: arr(a).reshape(-1, P).T

    def column(a):
        c = np.zeros((P, 1), f32)
        c[:SSD_HEADS, 0] = arr(a)[0]
        return c

    pos = np.arange(P)
    causal = (pos[:, None] <= pos[None, :]).astype(f32)
    tri = np.concatenate([causal, np.ones((P, P), f32), causal], axis=1)
    chunk = 64
    qc, kc = pos[:, None] // chunk, np.arange(T)[None, :] // chunk
    seen = np.concatenate([(kc[:, :P] <= qc) & (kc[:, :P] >= qc - 1),
                           (kc <= qc + 2) & (kc >= qc + 1)], axis=1)
    window = np.where(seen, f32(0), f32(-1e30)).astype(f32)
    parts = {
        "ones": np.ones((P, P), f32), "tri": tri, "window": window,
        "g1": cols(norm1_g), "g_mix": np.concatenate([cols(ssd_norm_g), arr(attn_norm_g)[0][att].reshape(-1, P).T], axis=1),
        "g2": cols(norm2_g), "d_skip": np.repeat(arr(d_skip)[0], HEAD_DIM).reshape(-1, P).T,
        "conv_w": arr(conv_w)[0].reshape(CONV_W, CONV_TILES, P).transpose(2, 1, 0).reshape(P, -1),
        "conv_b": cols(conv_b), "dt_bias": column(dt_bias), "a_log": column(a_log),
        "sinks": np.broadcast_to(arr(attn_sinks)[0][heads], (P, 2 * SSD_TILES)),
    }
    arrays = {
        "x_t": arr(x)[0].T.reshape(KT, P, T).transpose(1, 0, 2).reshape(P, KT * T),
        "small": np.concatenate([parts[n] for n in _small], axis=1),
        "id_iota": np.concatenate([np.eye(P, dtype=f32), np.broadcast_to(pos.astype(f32), (P, P))], axis=1),
        "w_in": chunks(wi),
        "w_out": chunks(wo),
        "w_q": chunks(arr(peer_wq)[0]),
        "keys": arr(peer_keys)[0].reshape(2 * PEER_HEADS, N_KEYS, P).transpose(2, 0, 1).reshape(P, -1),
        "u_tab": np.ascontiguousarray(arr(peer_u)[0].reshape(N_KEYS, P, KT, P).transpose(0, 3, 2, 1)).reshape(N_KEYS, P, D),
        "v_tab": arr(peer_v)[0].reshape(N_KEYS, P, D),
        "g_f": np.broadcast_to(arr(norm_f_g), (P, D)),
    }
    nc = bacc.Bacc("TRN2", target_bir_lowering=False, num_devices=1, dynamic_dma_scratch_size=4096)
    args = []
    for name in arrays:
        arrays[name] = np.ascontiguousarray(arrays[name])
        args.append(nc.dram_tensor(name, arrays[name].shape, F32, kind="ExternalInput").ap())
    args.append(nc.dram_tensor("out", (T, D), F32, kind="ExternalOutput").ap())
    build(nc, *args)
    r = run_bass_kernel_spmd(nc, [arrays], core_ids=[0])
    return r.results[0]["out"].reshape(1, T, D)
```
